# Optimizing a Trainium2 kernel written in Bass

```python
import jax, jax.numpy as jnp
from jax import lax
import numpy as np

D_MODEL = 1024
BATCH = 1
SEQ = 1024
DEPTH = 1

CHUNK = 64
HEAD_DIM = 64
EPS = 1e-6
NEG_INF = -1e30
GDN_HEADS = D_MODEL // (2 * HEAD_DIM)
GDN_WIDTH = GDN_HEADS * HEAD_DIM
GDN_CONV = 4
SWA_Q_HEADS = D_MODEL // (2 * HEAD_DIM)
SWA_KV_HEADS = SWA_Q_HEADS // 4
SWA_WIDTH = SWA_Q_HEADS * HEAD_DIM
SWA_KV_WIDTH = SWA_KV_HEADS * HEAD_DIM
SWA_WINDOW = 128
SWA_WIN_CHUNKS = -(-SWA_WINDOW // CHUNK)
REL_BUCKETS = 32
REL_MAX_DIST = 128
MIX_WIDTH = GDN_WIDTH + SWA_WIDTH
IN_SIZES = (GDN_WIDTH, GDN_WIDTH, GDN_WIDTH, GDN_WIDTH, GDN_HEADS, GDN_HEADS, SWA_WIDTH, SWA_KV_WIDTH, SWA_KV_WIDTH)
IN_WIDTH = 4 * GDN_WIDTH + 2 * GDN_HEADS + SWA_WIDTH + 2 * SWA_KV_WIDTH
PEER_HEADS = 8
PEER_NKEYS = 128
PEER_EXPERTS = PEER_NKEYS * PEER_NKEYS
PEER_TOPK = 16
PEER_KEY_HALF = 128
PEER_BLOCK = 128
PLE_DIM = 256

kernel_name = 'hybrid_gdn_swa_peer_block'

def rms_norm(x, g):
    xf = x.astype(jnp.float32)
    y = xf * lax.rsqrt(jnp.mean(xf * xf, axis=-1, keepdims=True) + EPS)
    return (y * g.astype(jnp.float32)).astype(x.dtype)

def l2_normalize(t):
    return t * lax.rsqrt(jnp.sum(t * t, axis=-1, keepdims=True) + EPS)

def causal_depthwise_conv(x, w):
    k_width, ch = w.shape
    return lax.conv_general_dilated(x, w[:, None, :].astype(x.dtype), window_strides=(1,), padding=((k_width - 1, 0),), dimension_numbers=('NWC', 'WIO', 'NWC'), feature_group_count=ch)

def to_chunks(t):
    b, s, h, d = t.shape
    return t.reshape(b, s // CHUNK, CHUNK, h, d).transpose(0, 1, 3, 2, 4)

def gated_delta_net(q, k, v, z, b_logit, a_logit, conv_w, a_log, dt_bias, norm_g):
    bsz, seq, _ = q.shape
    out_dtype = z.dtype
    f32 = jnp.float32
    qkv = jax.nn.silu(causal_depthwise_conv(jnp.concatenate([q, k, v], axis=-1), conv_w)).astype(f32)
    q, k, v = jnp.split(qkv, 3, axis=-1)
    hs = (bsz, seq, GDN_HEADS, HEAD_DIM)
    q = l2_normalize(q.reshape(hs)) * (HEAD_DIM ** -0.5)
    k = l2_normalize(k.reshape(hs))
    v = v.reshape(hs)
    beta = jax.nn.sigmoid(b_logit.astype(f32))
    g = -jnp.exp(a_log.astype(f32)) * jax.nn.softplus(a_logit.astype(f32) + dt_bias.astype(f32))
    qc, kc, vc = to_chunks(q), to_chunks(k), to_chunks(v)
    bc = to_chunks(beta[..., None])[..., 0]
    gc = jnp.cumsum(to_chunks(g[..., None])[..., 0], axis=-1)
    incl = np.tril(np.ones((CHUNK, CHUNK), dtype=bool))
    strict = np.tril(np.ones((CHUNK, CHUNK), dtype=bool), -1)
    decay = jnp.exp(jnp.where(incl, gc[..., :, None] - gc[..., None, :], -jnp.inf))
    kb = kc * bc[..., None]
    a_mat = jnp.where(strict, jnp.einsum('bnhid,bnhjd->bnhij', kb, kc) * decay, 0.0)
    eye = jnp.eye(CHUNK, dtype=f32)
    t_inv = lax.linalg.triangular_solve(a_mat + eye, jnp.broadcast_to(eye, a_mat.shape), left_side=True, lower=True, unit_diagonal=True)
    w_c = t_inv @ (kb * jnp.exp(gc)[..., None])
    u_c = t_inv @ (vc * bc[..., None])
    qk = jnp.einsum('bnhid,bnhjd->bnhij', qc, kc) * decay
    qg = qc * jnp.exp(gc)[..., None]
    kdec = kc * jnp.exp(gc[..., -1:] - gc)[..., None]
    glast = jnp.exp(gc[..., -1])

    def step(state, inp):
        w_n, u_n, qk_n, qg_n, kd_n, gl_n = inp
        v_new = u_n - jnp.einsum('bhck,bhkv->bhcv', w_n, state)
        o_n = jnp.einsum('bhck,bhkv->bhcv', qg_n, state) + jnp.einsum('bhij,bhjv->bhiv', qk_n, v_new)
        state = state * gl_n[..., None, None] + jnp.einsum('bhck,bhcv->bhkv', kd_n, v_new)
        return state, o_n

    xs = (jnp.moveaxis(w_c, 1, 0), jnp.moveaxis(u_c, 1, 0), jnp.moveaxis(qk, 1, 0), jnp.moveaxis(qg, 1, 0), jnp.moveaxis(kdec, 1, 0), jnp.moveaxis(glast, 1, 0))
    s0 = jnp.zeros((bsz, GDN_HEADS, HEAD_DIM, HEAD_DIM), f32)
    _, o = lax.scan(step, s0, xs)
    o = o.transpose(1, 0, 3, 2, 4).reshape(hs)
    o = rms_norm(o, norm_g) * jax.nn.silu(z.reshape(hs).astype(f32))
    return o.reshape(bsz, seq, GDN_WIDTH).astype(out_dtype)

def t5_relative_bucket(rel):
    half = REL_BUCKETS // 2
    max_exact = half // 2
    ret = (rel > 0).astype(np.int32) * half
    n = np.abs(rel)
    large = max_exact + (np.log(np.maximum(n, 1) / max_exact) / np.log(REL_MAX_DIST / max_exact) * (half - max_exact)).astype(np.int32)
    large = np.minimum(large, half - 1)
    return ret + np.where(n < max_exact, n, large).astype(np.int32)

def shift_chunks(tc, s):
    if s == 0:
        return tc
    return jnp.pad(tc, ((0, 0), (s, 0), (0, 0), (0, 0), (0, 0)))[:, :-s]

def sliding_window_attention(q, k, v, q_norm_g, k_norm_g, rel_bias, sinks):
    bsz, seq, _ = q.shape
    out_dtype = q.dtype
    f32 = jnp.float32
    n_chunks = seq // CHUNK
    groups = SWA_Q_HEADS // SWA_KV_HEADS
    span = SWA_WIN_CHUNKS * CHUNK
    q = rms_norm(q.reshape(bsz, seq, SWA_Q_HEADS, HEAD_DIM), q_norm_g) * (HEAD_DIM ** -0.5)
    k = rms_norm(k.reshape(bsz, seq, SWA_KV_HEADS, HEAD_DIM), k_norm_g)
    v = v.reshape(bsz, seq, SWA_KV_HEADS, HEAD_DIM)
    qb = q.reshape(bsz, n_chunks, CHUNK, SWA_KV_HEADS, groups, HEAD_DIM)

    def band(t):
        tc = t.reshape(bsz, n_chunks, CHUNK, SWA_KV_HEADS, HEAD_DIM)
        return jnp.concatenate([shift_chunks(tc, s) for s in range(SWA_WIN_CHUNKS - 1, -1, -1)], axis=2)

    kb, vb = band(k), band(v)
    logits = jnp.einsum('bnikgd,bnjkd->bnkgij', qb, kb, preferred_element_type=f32)
    q_off = np.arange(CHUNK)[:, None]
    k_off = np.arange(span)[None, :] - (SWA_WIN_CHUNKS - 1) * CHUNK
    buckets = t5_relative_bucket(k_off - q_off)
    bias = jnp.transpose(rel_bias.astype(f32)[buckets], (2, 0, 1)).reshape(SWA_KV_HEADS, groups, CHUNK, span)
    valid = (np.arange(n_chunks)[:, None] * CHUNK + k_off) >= 0
    logits = jnp.where(valid[None, :, None, None, None, :], logits + bias, NEG_INF)
    sink = sinks.astype(f32).reshape(1, 1, SWA_KV_HEADS, groups, 1)
    m = jnp.maximum(jnp.max(logits, axis=-1), sink)
    probs = jnp.exp(logits - m[..., None])
    denom = jnp.sum(probs, axis=-1) + jnp.exp(sink - m)
    out = jnp.einsum('bnkgij,bnjkd->bnikgd', probs / denom[..., None], vb.astype(f32))
    return out.reshape(bsz, seq, SWA_WIDTH).astype(out_dtype)

def peer_experts(xn, w_query, sub_keys, expert_u, expert_v):
    bsz, seq, dm = xn.shape
    f32 = jnp.float32
    xt = xn.reshape((bsz * seq) // PEER_BLOCK, PEER_BLOCK, dm)
    keys1 = sub_keys[0].astype(f32)
    keys2 = sub_keys[1].astype(f32)

    def block(xb):
        qr = (xb @ w_query).astype(f32).reshape(PEER_BLOCK, PEER_HEADS, 2, PEER_KEY_HALF)
        s1 = jnp.einsum('thd,hnd->thn', qr[:, :, 0], keys1)
        s2 = jnp.einsum('thd,hnd->thn', qr[:, :, 1], keys2)
        v1, i1 = lax.top_k(s1, PEER_TOPK)
        v2, i2 = lax.top_k(s2, PEER_TOPK)
        cand = (v1[..., :, None] + v2[..., None, :]).reshape(PEER_BLOCK, PEER_HEADS, PEER_TOPK * PEER_TOPK)
        sc, ci = lax.top_k(cand, PEER_TOPK)
        e1 = jnp.take_along_axis(i1, ci // PEER_TOPK, axis=-1)
        e2 = jnp.take_along_axis(i2, ci % PEER_TOPK, axis=-1)
        eid = e1 * PEER_NKEYS + e2
        gate = jax.nn.softmax(sc, axis=-1)
        hid = jnp.einsum('thkd,td->thk', expert_u[eid], xb, preferred_element_type=f32)
        act = jax.nn.gelu(hid, approximate=False) * gate
        return jnp.einsum('thk,thkd->td', act, expert_v[eid].astype(f32)).astype(xb.dtype)

    return lax.map(block, xt).reshape(bsz, seq, dm)

def setup_inputs(seed: int = 0) -> dict:
    key = jax.random.key(seed)
    ks = jax.random.split(key, 21)
    f32 = jnp.float32
    L = DEPTH

    def nrm(k, shape, scale):
        return jax.random.normal(k, shape, f32) * scale

    def gain(k, shape):
        return 1.0 + 0.05 * jax.random.normal(k, shape, f32)

    return {
        'x': nrm(ks[0], (BATCH, SEQ, D_MODEL), 1.0),
        'p': nrm(ks[1], (DEPTH, BATCH, SEQ, PLE_DIM), 1.0),
        'g_mix': gain(ks[2], (L, D_MODEL)),
        'w_in': nrm(ks[3], (L, D_MODEL, IN_WIDTH), D_MODEL ** -0.5),
        'gdn_conv_w': nrm(ks[4], (L, GDN_CONV, 3 * GDN_WIDTH), GDN_CONV ** -0.5),
        'gdn_a_log': jnp.log(jax.random.uniform(ks[5], (L, GDN_HEADS), f32, 1.0, 16.0)),
        'gdn_dt_bias': jnp.log(jnp.expm1(jax.random.uniform(ks[6], (L, GDN_HEADS), f32, 1e-3, 0.1))),
        'gdn_norm_g': gain(ks[7], (L, HEAD_DIM)),
        'swa_q_norm_g': gain(ks[8], (L, HEAD_DIM)),
        'swa_k_norm_g': gain(ks[9], (L, HEAD_DIM)),
        'swa_sinks': nrm(ks[10], (L, SWA_Q_HEADS), 0.5),
        'rel_bias': nrm(ks[11], (REL_BUCKETS, SWA_Q_HEADS), 0.1),
        'w_out': nrm(ks[12], (L, MIX_WIDTH, D_MODEL), MIX_WIDTH ** -0.5),
        'g_ffn': gain(ks[13], (L, D_MODEL)),
        'peer_w_query': nrm(ks[14], (L, D_MODEL, PEER_HEADS * 2 * PEER_KEY_HALF), D_MODEL ** -0.5),
        'peer_sub_keys': nrm(ks[15], (L, 2, PEER_HEADS, PEER_NKEYS, PEER_KEY_HALF), PEER_KEY_HALF ** -0.5),
        'peer_u': nrm(ks[16], (L, PEER_EXPERTS, D_MODEL), D_MODEL ** -0.5),
        'peer_v': nrm(ks[17], (L, PEER_EXPERTS, D_MODEL), 0.3),
        'g_ple': gain(ks[18], (L, D_MODEL)),
        'ple_w_gate': nrm(ks[19], (L, D_MODEL, D_MODEL), D_MODEL ** -0.5),
        'ple_w_proj': nrm(ks[20], (L, PLE_DIM, D_MODEL), PLE_DIM ** -0.5),
    }

def reference(x, p, g_mix, w_in, gdn_conv_w, gdn_a_log, gdn_dt_bias, gdn_norm_g, swa_q_norm_g, swa_k_norm_g, swa_sinks, rel_bias, w_out, g_ffn, peer_w_query, peer_sub_keys, peer_u, peer_v, g_ple, ple_w_gate, ple_w_proj):
    h = x
    cuts = np.cumsum(IN_SIZES)[:-1].tolist()
    for i in range(DEPTH):
        n = rms_norm(h, g_mix[i])
        proj = n @ w_in[i]
        gq, gk, gv, gz, gb, ga, sq, sk, sv = jnp.split(proj, cuts, axis=-1)
        o_gdn = gated_delta_net(gq, gk, gv, gz, gb, ga, gdn_conv_w[i], gdn_a_log[i], gdn_dt_bias[i], gdn_norm_g[i])
        o_swa = sliding_window_attention(sq, sk, sv, swa_q_norm_g[i], swa_k_norm_g[i], rel_bias, swa_sinks[i])
        h = h + (jnp.concatenate([o_gdn, o_swa], axis=-1) @ w_out[i]).astype(h.dtype)
        h = h + peer_experts(rms_norm(h, g_ffn[i]), peer_w_query[i], peer_sub_keys[i], peer_u[i], peer_v[i]).astype(h.dtype)
        gate = jax.nn.sigmoid(rms_norm(h, g_ple[i]) @ ple_w_gate[i])
        h = h + (gate * (p[i] @ ple_w_proj[i])).astype(h.dtype)
    return h


_drawn_inputs = setup_inputs


def setup_inputs(seed=0):
    import zlib

    import numpy as np

    out = dict(_drawn_inputs(seed))
    spreads = {}
    factors = {'swa_q_norm_g': 5.724,
     'swa_k_norm_g': 5.395,
     'swa_sinks': 8.0,
     'rel_bias': 3.615,
     'g_ple': 6.711}
    for name, (base, spread) in spreads.items():
        noise = np.random.default_rng([zlib.crc32(name.encode()), seed]).standard_normal(out[name].shape)
        drawn = base * np.exp(spread * noise) if base else spread * noise
        out[name] = __import__('jax').numpy.asarray(drawn.astype(out[name].dtype))
    for name, factor in factors.items():
        out[name] = (out[name] * factor).astype(out[name].dtype)
    return out
```

```python
from contextlib import ExitStack

import numpy as np

import concourse.bass as bass
from concourse import mybir

ALU = mybir.AluOpType
ACT = mybir.ActivationFunctionType
AX = mybir.AxisListType
F32 = mybir.dt.float32
U32 = mybir.dt.uint32

P = 128
D = 1024
DC = D // P
SEQ = 1024
NT = SEQ // P
CHUNK = 64
HD = 64
NH = 8
NKV = 2
GW = NH * HD
QKV = 3 * GW
TOKW = 2832 - QKV
Z0, B0, A0, SQ0, SK0, SV0 = 0, 512, 520, 528, 1040, 1168
CONV = 4
WIN = CHUNK + P
LEVELS = 6
EPS = 1e-6
MASKED = -1e30
REL_BUCKETS, REL_MAX_DIST = 32, 128
RELS = 320
PLE = 256
PH = 8
NKEYS = 128
TOPK = 16
NHH = 2 * PH
SLOTS = PH * TOPK
G = 8
NG = SLOTS // G
QCOL = 256
NQ = PH * 2 * 128 // QCOL
LEAST = -3.0e38
V_STEPS = 143

C_ID, C_TRIL, C_BLOCK, C_ONES, C_CH0, C_CH1 = (P * i for i in range(6))
C_LEVEL = 6 * P
C_WIN = C_LEVEL + LEVELS * P
C_IOTA = C_WIN + WIN
C_REL = C_IOTA + TOPK
C_ALL = C_REL + RELS


def t5_bucket(rel):
    half = REL_BUCKETS // 2
    exact = half // 2
    n = np.abs(rel)
    large = exact + (np.log(np.maximum(n, 1) / exact) / np.log(REL_MAX_DIST / exact) * (half - exact)).astype(np.int32)
    return (rel > 0).astype(np.int32) * half + np.where(n < exact, n, np.minimum(large, half - 1)).astype(np.int32)


def constants():
    c = np.zeros((P, C_ALL), np.float32)
    i = np.arange(P)
    row, col = i[:, None], i[None, :]
    same = row // CHUNK == col // CHUNK
    c[:, C_ID:C_ID + P] = row == col
    c[:, C_TRIL:C_TRIL + P] = same & (row <= col)
    c[:, C_BLOCK:C_BLOCK + P] = same
    c[:, C_ONES:C_ONES + P] = 1.0
    c[:CHUNK, C_CH0:C_CH0 + P] = 1.0
    c[CHUNK:, C_CH1:C_CH1 + P] = 1.0
    for l in range(LEVELS):
        at = C_LEVEL + l * P
        c[:, at:at + P] = (row >> (l + 1) == col >> (l + 1)) & ((col >> l) & 1 == 1) & ((row >> l) & 1 == 0)
    w = np.arange(WIN)[None, :]
    seen = np.where(row < CHUNK, w < 2 * CHUNK, w >= CHUNK)
    c[:, C_WIN:C_WIN + WIN] = np.where(seen, 0.0, MASKED)
    c[:, C_IOTA:C_IOTA + TOPK] = np.arange(TOPK)
    rel = np.arange(RELS) - (WIN - 1)
    c[:REL_BUCKETS, C_REL:C_REL + RELS] = t5_bucket(rel)[None, :] == np.arange(REL_BUCKETS)[:, None]
    return c


def block_kernel(nc, x, p, g_mix, w_in, gdn_conv_w, gdn_a_log, gdn_dt_bias, gdn_norm_g, swa_q_norm_g, swa_k_norm_g,
                 swa_sinks, rel_bias, w_out, g_ffn, peer_w_query, peer_sub_keys, peer_u, peer_v, g_ple, ple_w_gate,
                 ple_w_proj, consts, out):
    x, p, out = x[0], p[0, 0], out[0]
    w_in, w_out, w_query = w_in[0], w_out[0], peer_w_query[0]
    sub_keys, table_u, table_v = peer_sub_keys[0], peer_u[0], peer_v[0]
    w_gate, w_proj, conv_w = ple_w_gate[0], ple_w_proj[0], gdn_conv_w[0]

    conv_dram = nc.dram_tensor("conv_scratch", (QKV, SEQ), F32, kind="Internal").ap()
    tok_dram = nc.dram_tensor("tok_scratch", (SEQ, TOKW), F32, kind="Internal").ap()
    h1_dram = nc.dram_tensor("h1_scratch", (SEQ, D), F32, kind="Internal").ap()
    h2_dram = nc.dram_tensor("h2_scratch", (SEQ, D), F32, kind="Internal").ap()
    rel_dram = nc.dram_tensor("rel_scratch", (NH, P, RELS), F32, kind="Internal").ap()

    with ExitStack() as ctx:
        def signal(name):
            return ctx.enter_context(nc.semaphore(name))

        consts_loaded = signal("consts_loaded")
        params_a = signal("params_a")
        a_w_loaded = signal("a_w_loaded")
        params_b = signal("params_b")
        a_tok_ready = signal("a_tok_ready")
        a_n_ready = signal("a_n_ready")
        a_conv_ready = signal("a_conv_ready")
        a_conv_stored = [signal(f"a_conv_stored{u}") for u in range(2)]
        a_channels_mm = signal("a_channels_mm")
        a_nT_ready = signal("a_nT_ready")
        a_nT_copied = signal("a_nT_copied")
        a_tok_mm = signal("a_tok_mm")
        a_halo_zero = signal("a_halo_zero")
        a_in_ready = signal("a_in_ready")
        a_conv_sum = signal("a_conv_sum")
        a_turned = signal("a_turned")
        inverse_root = signal("inverse_root")
        keys_loaded = signal("keys_loaded")
        w_out_loaded = signal("w_out_loaded")
        rel_rows_ready = signal("rel_rows_ready")
        rel_stored = signal("rel_stored")
        bias_loaded = signal("bias_loaded")
        keysT_ready = signal("keysT_ready")
        keys_T = signal("keys_T")
        rel_mm = signal("rel_mm")
        rate_exp = signal("rate_exp")
        rate_ready = signal("rate_ready")
        bias_ready = signal("bias_ready")
        c_w_loaded = signal("c_w_loaded")
        c_out_ready = signal("c_out_ready")
        c_gate = signal("c_gate")
        c_pT_turned = signal("c_pT_turned")
        c_pT_ready = signal("c_pT_ready")
        c_proj_mm = signal("c_proj_mm")
        c_gated = signal("c_gated")
        gelu = signal("gelu")
        ids_taken = signal("ids_taken")
        inputs_ready = signal("inputs_ready")
        h2_stored = signal("h2_stored")
        residual_loaded = signal("residual_loaded")
        h2_ready = signal("h2_ready")
        group_ids_ready = signal("group_ids_ready")
        u_used = signal("u_used")
        u_landed = [signal(f"u_landed{u}") for u in range(G)]
        v_used = signal("v_used")
        v_landed = [signal(f"v_landed{u}") for u in range(G)]
        weights_ready = signal("weights_ready")
        diag_ready = signal("diag_ready")
        s_exp = signal("s_exp")
        rows_in = [signal(f"rows_in{u}") for u in range(2)]
        rows_stored = [signal(f"rows_stored{u}") for u in range(2)]
        wq_loaded = [signal(f"wq_loaded{u}") for u in range(2)]
        vector_front = signal("vector_front")
        h1_stored = signal("h1_stored")
        qkv_loaded = signal("qkv_loaded")
        tok_loaded = signal("tok_loaded")
        squares = signal("squares")
        s_T = signal("s_T")
        s_T_out = signal("s_T_out")
        x_loaded = signal("x_loaded")
        h1_ready = signal("h1_ready")
        query_mm = signal("query_mm")
        row_squares = signal("row_squares")
        mean_square = signal("mean_square")
        root = signal("root")
        qkv_tok = signal("qkv_tok")
        beta_exp = signal("beta_exp")
        x_abs = signal("x_abs")
        x_exp = signal("x_exp")
        softplus_tail = signal("softplus_tail")
        gcs_ready = signal("gcs_ready")
        k_gap = signal("k_gap")
        decays = signal("decays")
        dec_arg = signal("dec_arg")
        dec_exp = signal("dec_exp")
        heads_T = signal("heads_T")
        heads_T_out = signal("heads_T_out")
        inv_turned = signal("inv_turned")
        inv_ready = signal("inv_ready")
        qkT_ready = signal("qkT_ready")
        level_x = signal("level_x")
        level_x_out = signal("level_x_out")
        nw_mm = signal("nw_mm")
        nw_out = signal("nw_out")
        u_mm = signal("u_mm")
        u_out = signal("u_out")
        silu_z = signal("silu_z")
        o_inter_mm = signal("o_inter_mm")
        o_inter_out = signal("o_inter_out")
        o_sum = signal("o_sum")
        o_squares = signal("o_squares")
        o_T = signal("o_T")
        mix_ready = signal("mix_ready")
        s_squares = signal("s_squares")
        window_moved = signal("window_moved")
        s_max = signal("s_max")
        probs_T = signal("probs_T")
        probsT_ready = signal("probsT_ready")
        av_mm = signal("av_mm")
        n2_T = signal("n2_T")
        n2T_ready = signal("n2T_ready")
        qr_ready = signal("qr_ready")
        qr_T = signal("qr_T")
        qrT_ready = signal("qrT_ready")
        score_mm = signal("score_mm")
        scores_ready = signal("scores_ready")
        gate_arg = signal("gate_arg")
        gate_exp = signal("gate_exp")
        g_ready = signal("g_ready")
        h1_mm = signal("h1_mm")
        cumsum = signal("cumsum")
        gdiag_ready = signal("gdiag_ready")
        gc_rows = signal("gc_rows")
        scaled = signal("scaled")
        invT_ready = signal("invT_ready")
        kk_mm = signal("kk_mm")
        qk_mm = signal("qk_mm")
        level_p = signal("level_p")
        state_ready = signal("state_ready")
        ws_mm = signal("ws_mm")
        v_new_ready = signal("v_new_ready")
        kv_mm = signal("kv_mm")
        o_intra_mm = signal("o_intra_mm")
        o_normed = signal("o_normed")
        s_normed = signal("s_normed")
        logits_mm = signal("logits_mm")
        probs_ready = signal("probs_ready")
        xb_ready = signal("xb_ready")
        vector_step = signal("vector_step")
        wait_carrier = signal("wait_carrier")

        def sb(where, name, shape, dt=F32):
            return where.enter_context(nc.sbuf_tensor(name, shape, dt))


        bank = [ctx.enter_context(nc.psum_tensor(f"bank{i}", [P, 512], F32)) for i in range(6)]
        acc = ctx.enter_context(nc.psum_tensor("expert_sum", [P, D], F32))

        cst = sb(ctx, "constants", [P, C_ALL])
        ident = cst[:, C_ID:C_ID + P]
        g_mix_c = sb(ctx, "g_mix_by_channel", [P, DC])
        conv_c = sb(ctx, "conv_by_channel", [P, CONV, QKV // P])
        q_gain = sb(ctx, "swa_q_gain", [P, 1])
        k_gain = sb(ctx, "swa_k_gain", [P, 1])
        norm_g = sb(ctx, "gdn_norm_gain", [P, HD])
        a_rate = sb(ctx, "a_log_rows", [P, NH])
        neg_rate = sb(ctx, "minus_exp_a_log", [P, NH])
        dt_row = sb(ctx, "dt_bias_rows", [P, NH])
        sinks = sb(ctx, "sink_rows", [P, NH])
        small = sb(ctx, "small", [P, 280])
        rel_sb = sb(ctx, "rel_bias_sb", [REL_BUCKETS, NH])
        bias_t = sb(ctx, "swa_bias", [P, NH, WIN])

        with ExitStack() as a_ctx:
            a_w = sb(a_ctx, "w_token", [P, DC, TOKW])
            a_nT = sb(a_ctx, "normed_by_channel", [P, DC, SEQ])
            a_x = [sb(a_ctx, f"x_in{u}", [P, D]) for u in range(2)]
            a_n = [sb(a_ctx, f"x_normed{u}", [P, D]) for u in range(2)]
            a_nTt = [sb(a_ctx, f"normed_tile{u}", [P, DC, P]) for u in range(2)]
            a_tok = [sb(a_ctx, f"token_out{u}", [P, TOKW]) for u in range(2)]
            a_wc = [sb(a_ctx, f"w_channel{u}", [P, DC, P]) for u in range(2)]
            a_in = [sb(a_ctx, f"conv_in{u}", [P, CONV - 1 + SEQ]) for u in range(2)]
            a_cv = [sb(a_ctx, f"conv_sum{u}", [P, SEQ]) for u in range(2)]
            a_out = [sb(a_ctx, f"conv_out{u}", [P, SEQ]) for u in range(2)]
        with ExitStack() as b_ctx:
            w_out_sb = sb(b_ctx, "w_out_sb", [P, DC, D])
            keysT = sb(b_ctx, "keys_by_channel", [P, NHH, P])
            wq = [sb(b_ctx, f"w_query{u}", [P, DC, QCOL]) for u in range(2)]
            u_ring = sb(b_ctx, "u_rows", [P, G, D])
            v_ring = sb(b_ctx, "v_rows", [P, G, D])
            g_ffn_b = sb(b_ctx, "g_ffn_rows", [P, D])
            xb_new = sb(b_ctx, "ffn_in_new", [P, D])
            xb = sb(b_ctx, "ffn_in", [P, D])
            h_res = xb_new
            eid_new = sb(b_ctx, "expert_id_new", [P, SLOTS])
            eid = sb(b_ctx, "expert_id", [P, SLOTS], U32)
            gate_new = sb(b_ctx, "gate_new", [P, SLOTS])
            gate = sb(b_ctx, "gate", [P, SLOTS])
            hid = sb(b_ctx, "hidden", [P, SLOTS])
            gel = sb(b_ctx, "gelu", [P, SLOTS])
            act_w = sb(b_ctx, "expert_weight", [P, SLOTS])
            ids = sb(b_ctx, "group_ids", [P, 2, G], U32)
            diag = sb(b_ctx, "weight_diagonals", [P, G, P])
            state = sb(b_ctx, "gdn_state", [P, 4, HD])
            kwin = sb(b_ctx, "key_window", [P, WIN])
            vprev = sb(b_ctx, "values_before", [P, P])
            vcur = sb(b_ctx, "values_here", [P, P])
            KB = 256
            arena = sb(b_ctx, "arena", [P, 49 * KB + 64])
            keys_in = u_ring[:, 0:2, :].rearrange("p a (b n) -> p (a b) n", n=P)
            rel_rows = v_ring[:].rearrange("p a n -> p (a n)")[:, 0:NH * RELS].rearrange("p (h r) -> p h r", h=NH)
        with ExitStack() as c_ctx:
            wg_sb = sb(c_ctx, "w_gate_sb", [P, DC, D])
            wp_sb = sb(c_ctx, "w_proj_sb", [P, PLE // P, D])
            g_ple_b = sb(c_ctx, "g_ple_rows", [P, D])
            c_h = [sb(c_ctx, f"h2_in{u}", [P, D]) for u in range(2)]
            c_p = [sb(c_ctx, f"p_in{u}", [P, PLE]) for u in range(2)]
            c_n = sb(c_ctx, "ple_normed", [P, D])
            c_nT = sb(c_ctx, "ple_normed_T", [P, DC, P])
            c_pT = sb(c_ctx, "p_T", [P, PLE // P, P])
            c_e = sb(c_ctx, "ple_exp", [P, D])
            c_o = [sb(c_ctx, f"ple_out{u}", [P, D]) for u in range(2)]
            c_junk = sb(c_ctx, "ple_junk", [P, D])

        def part(kb, cols):
            return arena[:, int(kb * KB):int(kb * KB) + cols]

        qkv_in = part(0, QKV).rearrange("p (c n) -> p c n", n=P)
        tokp = part(6, TOKW)
        x_t = part(2, D)
        kn, nkb, qn, qg = (part(11.25 + 2 * i, GW) for i in range(4))
        vb, nkbg, kdec = (part(19.25 + 2 * i, GW) for i in range(3))
        knT, nkbT, qnT, qgT = (part(25.25 + 2 * i, GW).rearrange("p (q n) -> p q n", n=P) for i in range(4))
        decT = part(33.25, 8 * P).rearrange("p (s n) -> p s n", n=P)
        amT = part(37.25, 8 * P).rearrange("p (s n) -> p s n", n=P)
        square = part(37.25, 8 * P)
        qkT = part(41.25, 8 * P).rearrange("p (s n) -> p s n", n=P)
        gdiag = part(41.25, 8 * P).rearrange("p (s n) -> p s n", n=P)
        mixT = part(45.25, 8 * P).rearrange("p (s n) -> p s n", n=P)
        invT = part(11.25, 8 * P).rearrange("p (s n) -> p s n", n=P)
        step_x = part(15.25, 8 * P).rearrange("p (s n) -> p s n", n=P)
        inv = decT
        nwT, u_sb, v_new, o_inter = knT, part(27.25, GW), part(29.25, GW), part(0, GW)
        o_sb, zs, o_sq = part(2, GW), part(4, GW), part(15.25, GW)
        s_n = part(0, 10 * HD)
        s_sq = part(3, 10 * HD)
        sqT = part(19.25, GW).rearrange("p (q n) -> p q n", n=P)
        probs = part(11.25, NH * 256).rearrange("p (h n) -> p h n", n=256)
        probsT = part(25.25, 16 * P).rearrange("p (s n) -> p s n", n=P)
        h1 = part(11.25, D)
        n2T = part(15.25, D).rearrange("p (c n) -> p c n", n=P)
        h_junk = part(0, D)
        qr, qrT = part(19.25, QCOL), part(20.25, QCOL).rearrange("p (s n) -> p s n", n=P)
        scores = part(25.25, NHH * P).rearrange("p (s n) -> p s n", n=P)
        cand = part(33.25, PH * 256).rearrange("p (h n) -> p h n", n=256)
        onehot = part(41.25, 2 * D).rearrange("p (h k a) -> p h k a", h=PH, k=TOPK)
        vtop = part(4, NHH * TOPK).rearrange("p (s k) -> p s k", k=TOPK)
        itop = part(5, NHH * TOPK).rearrange("p (s k) -> p s k", k=TOPK).bitcast(U32)
        itop_f = part(6, NHH * TOPK).rearrange("p (s k) -> p s k", k=TOPK)
        ctop = part(7, SLOTS).rearrange("p (h k) -> p h k", k=TOPK)
        cidx = part(7.5, SLOTS).rearrange("p (h k) -> p h k", k=TOPK).bitcast(U32)
        chalf = part(8, SLOTS).rearrange("p (h k) -> p h k", k=TOPK).bitcast(U32)
        chalf_f = part(8.5, 2 * SLOTS).rearrange("p (f s) -> p f s", f=2)
        e_half = part(9.5, 2 * SLOTS).rearrange("p (f s) -> p f s", f=2)
        ssq, rst = small[:, 0:16], small[:, 16:32]
        beta, nbeta, gl, eg, kd = (small[:, 32 + 8 * i:40 + 8 * i] for i in range(5))
        xa, xabs, e2 = (small[:, 72 + 8 * i:80 + 8 * i] for i in range(3))
        gcs = small[:, 96:128]
        glp = small[:, 128:136].rearrange("p (c q) -> p c q", c=2)
        kgap = small[:, 136:144]
        s_ss, s_rs = small[:, 144:154], small[:, 154:164]
        s_m, s_nm, s_den, s_es, s_gap = (small[:, 164 + 8 * i:172 + 8 * i] for i in range(5))
        h_ss, h_rs = small[:, 204:205], small[:, 205:206]
        g_sum, g_inv = small[:, 206:214], small[:, 214:222]
        o_ss, o_rs = small[:, 222:230], small[:, 230:238]
        a_ss, a_rs = small[:, 240:242], small[:, 248:250]
        c_ss, c_rs = small[:, 256:257], small[:, 257:258]
        spl = small[:, 260:268]
        eb = small[:, 268:276]

        def heads(ap, n=NH):
            return ap.rearrange("p (h d) -> p h d", h=n)

        def per_head(ap, n=NH, width=HD):
            return ap.unsqueeze(2).broadcast_to([P, n, width])

        def norm_of(t, i):
            return NT + 4 * t + i

        block = ctx.enter_context(nc.Block())
        bias_banks = (3, 4, 5, 0)

        @block.sync
        def _(sp):
            sp.dma_start(cst[:], consts).then_inc(consts_loaded, 16)
            for u in range(2):
                sp.dma_start(a_x[u][:], x[u * P:u * P + P, :]).then_inc(rows_in[u], 16)
            with nc.allow_non_contiguous_dma("vectors of parameters, a few KB, loaded once"):
                sp.dma_start(g_mix_c[:], g_mix[0].rearrange("(c p) -> p c", p=P)).then_inc(params_a, 16)
                w_in_v = w_in.rearrange("(c p) n -> p c n", p=P)
                for c in range(4):
                    sp.dma_start(a_w[:, 2 * c:2 * c + 2, :], w_in_v[:, 2 * c:2 * c + 2, QKV:QKV + TOKW]).then_inc(a_w_loaded, 16)
                for k in range(CONV):
                    sp.dma_start(conv_c[:, k, :], conv_w[k].rearrange("(c p) -> p c", p=P)).then_inc(params_a, 16)
                for kv in range(NKV):
                    sp.dma_start(q_gain[kv * HD:kv * HD + HD, :], swa_q_norm_g.rearrange("a d -> d a")).then_inc(params_b, 16)
                    sp.dma_start(k_gain[kv * HD:kv * HD + HD, :], swa_k_norm_g.rearrange("a d -> d a")).then_inc(params_b, 16)
            sp.dma_start(norm_g[:], gdn_norm_g.broadcast_to([P, HD])).then_inc(params_b, 16)
            sp.dma_start(a_rate[:], gdn_a_log.broadcast_to([P, NH])).then_inc(params_b, 16)
            sp.dma_start(dt_row[:], gdn_dt_bias.broadcast_to([P, NH])).then_inc(params_b, 16)
            sp.dma_start(sinks[:], swa_sinks.broadcast_to([P, NH])).then_inc(params_b, 16)
            sp.dma_start(rel_sb[:], rel_bias).then_inc(params_b, 16)

            def store_tokens(t, u):
                sp.wait_ge(a_tok_ready, (t + u + 1) * 3)
                sp.dma_start(tok_dram[bass.ds((t + u) * P, P), :], a_tok[u][:]).then_inc(rows_stored[u], 16)

            with sp.Fori(0, NT // 2 - 1) as pair:
                t = pair * 2
                for u in range(2):
                    sp.wait_ge(a_n_ready, t + u + 1)
                    sp.dma_start(a_x[u][:], x[bass.ds((t + u + 2) * P, P), :]).then_inc(rows_in[u], 16)
                    store_tokens(t, u)
            for u in range(2):
                sp.dma_start(a_wc[u][:], w_in_v[:, :, u * P:u * P + P]).then_inc(wq_loaded[u], 16)
            for u in range(2):
                store_tokens(NT - 2, u)

            def store_channels(ct, u):
                sp.wait_ge(a_conv_ready, ct + u + 1)
                sp.dma_start(conv_dram[bass.ds((ct + u) * P, P), :], a_out[u][:]).then_inc(a_conv_stored[u], 16)

            with sp.Fori(0, QKV // P // 2 - 1) as pair:
                ct = pair * 2
                for u in range(2):
                    sp.wait_ge(a_channels_mm, (ct + u + 1) * 2)
                    sp.dma_start(a_wc[u][:], w_in_v[:, :, bass.ds((ct + u + 2) * P, P)]).then_inc(wq_loaded[u], 16)
                    store_channels(ct, u)
            for u in range(2):
                store_channels(QKV // P - 2, u)
            for u in range(2):
                sp.wait_ge(rows_stored[u], 16 * NT // 2)
                sp.wait_ge(a_conv_stored[u], 16 * QKV // P // 2)

            sp.dma_start(keys_in, sub_keys.rearrange("f h n d -> n (f h) d")).then_inc(keys_loaded, 16)
            sp.dma_start(w_out_sb[:], w_out.rearrange("(c p) n -> p c n", p=P)).then_inc(w_out_loaded, 16)
            sp.dma_start(g_ffn_b[:], g_ffn.broadcast_to([P, D])).then_inc(w_out_loaded, 16)
            sp.wait_ge(rel_rows_ready, NH)
            sp.dma_start(rel_dram.rearrange("h p r -> p h r"), rel_rows).then_inc(rel_stored, 16)
            sp.wait_ge(rel_stored, 16)
            sp.dma_start(bias_t[:], bass.AP(tensor=rel_dram.tensor, offset=WIN - 1 - CHUNK,
                                    ap=[[RELS - 1, P], [P * RELS, NH], [1, WIN]])).then_inc(bias_loaded, 16)

            def experts_residual(t):
                sp.wait_ge(inputs_ready, min(t + 2, NT) if isinstance(t, int) else t + 2)
                sp.wait_ge(h2_stored, t * 16)
                sp.wait_ge(h1_stored, (t + 1) * 16)
                sp.dma_start(h_res[:], h1_dram[bass.ds(t * P, P), :]).then_inc(residual_loaded, 16)

            def experts_store(t):
                sp.wait_ge(h2_ready, (t + 1) * 2)
                sp.dma_start(h2_dram[bass.ds(t * P, P), :], h_res[:]).then_inc(h2_stored, 16)

            def front_loads(t):
                at = bass.ds(t * P, P)
                sp.wait_ge(vector_front, t)
                sp.sem_inc(wait_carrier)
                sp.wait_ge(h1_stored, t * 16)
                sp.sem_inc(wait_carrier)
                sp.dma_start(qkv_in, conv_dram.rearrange("(c p) n -> p c n", p=P)[:, :, at]).then_inc(qkv_loaded, 16)
                sp.dma_start(tokp, tok_dram[at, :]).then_inc(tok_loaded, 16)
                for i in range(NQ):
                    if i == 1:
                        if not isinstance(t, int) or t >= 2:
                            experts_residual(t - 2)
                            experts_store(t - 2)
                        sp.wait_ge(s_T_out, 2 * t + 2)
                        sp.dma_start(x_t, x[at, :]).then_inc(x_loaded, 16)
                    if i == 2:
                        sp.wait_ge(h1_ready, (t + 1) * 2)
                        sp.dma_start(h1_dram[at, :], h1).then_inc(h1_stored, 16)
                    if i >= 2:
                        sp.wait_ge(query_mm, t * NQ + i - 1)
                    sp.dma_start(wq[i % 2][:], w_query.rearrange("(c p) n -> p c n", p=P)[:, :, i * QCOL:(i + 1) * QCOL]
                                 ).then_inc(wq_loaded[i % 2], 16)

            front_loads(0)
            front_loads(1)
            with sp.Fori(2, NT) as t:
                front_loads(t)
            for t in (NT - 2, NT - 1):
                experts_residual(t)
                experts_store(t)

            sp.wait_ge(h2_stored, 16 * NT)
            sp.dma_start(wg_sb[:], w_gate.rearrange("(c p) n -> p c n", p=P)).then_inc(c_w_loaded, 16)
            sp.dma_start(wp_sb[:], w_proj.rearrange("(c p) n -> p c n", p=P)).then_inc(c_w_loaded, 16)
            sp.dma_start(g_ple_b[:], g_ple.broadcast_to([P, D])).then_inc(c_w_loaded, 16)
            for u in range(2):
                sp.dma_start(c_h[u][:], h2_dram[u * P:u * P + P, :]).then_inc(rows_in[u], 16)
                sp.dma_start(c_p[u][:], p[u * P:u * P + P, :]).then_inc(rows_in[u], 16)

            def store_out(t, u):
                sp.wait_ge(c_out_ready, t + u + 1)
                sp.dma_start(out[bass.ds((t + u) * P, P), :], c_o[u][:]).then_inc(rows_stored[u], 16)

            with sp.Fori(0, NT // 2 - 1) as pair:
                t = pair * 2
                for u in range(2):
                    store_out(t, u)
                    sp.dma_start(c_h[u][:], h2_dram[bass.ds((t + u + 2) * P, P), :]).then_inc(rows_in[u], 16)
                    sp.dma_start(c_p[u][:], p[bass.ds((t + u + 2) * P, P), :]).then_inc(rows_in[u], 16)
            for u in range(2):
                store_out(NT - 2, u)
            for u in range(2):
                sp.wait_ge(rows_stored[u], 16 * NT)

        @block.gpsimd
        def _(pool):
            def gather_group(t, g, half):
                n = t * SLOTS + g * G
                first = isinstance(g, int) and g == 0 and isinstance(t, int)
                nc.gpsimd.tensor_copy(ids[:, half, :], eid[:, bass.ds(g * G, G)]).then_inc(group_ids_ready, 1)
                pool.wait_ge(group_ids_ready, t * NG + g + 1)
                pool.sem_inc(wait_carrier)
                for table, ring, used, landed in ((table_u, u_ring, u_used, u_landed), (table_v, v_ring, v_used, v_landed)):
                    for j in range(G):
                        if j % 2 == 0 and not first:
                            pool.wait_ge(used, n - G + j + 2)
                            pool.sem_inc(wait_carrier)
                        nc.gpsimd.indirect_dma_start(
                            ring[:, j, :], None, table, bass.IndirectOffsetOnAxis(ids[:, half, j:j + 1], 0)).then_inc(landed[j], 16)

            pool.wait_ge(keysT_ready, 4)
            pool.wait_ge(rel_stored, 16)
            def take_ids(t):
                pool.wait_ge(vector_front, t + 1)
                pool.sem_inc(wait_carrier)
                nc.gpsimd.tensor_copy(eid[:], eid_new[:]).then_inc(ids_taken, 1)
                pool.wait_ge(ids_taken, t + 1)

            take_ids(0)
            for half in range(2):
                gather_group(0, half, half)
            with pool.Fori(1, NG // 2) as pair:
                g = pair * 2
                for half in range(2):
                    gather_group(0, g + half, half)
            with pool.Fori(1, NT) as t:
                take_ids(t)
                pool.sem_inc(wait_carrier)
                with pool.Fori(0, NG // 2) as pair:
                    g = pair * 2
                    for half in range(2):
                        gather_group(t, g + half, half)

        @block.scalar
        def _(act):
            def f(out_, in_, func, **kw):
                return nc.scalar.activation(out_, in_, func, **kw)

            def token_pair(t):
                for u in range(2):
                    act.wait_ge(rows_in[u], t * 8 + 16)
                    f(a_cv[u][:], a_x[u][:], ACT.Square, accum_out=a_ss[:, u:u + 1]).then_inc(row_squares, 1)
                    act.wait_ge(mean_square, t + u + 1)
                    f(a_rs[:, u:u + 1], a_rs[:, u:u + 1], ACT.Sqrt).then_inc(root, 1)
                    act.wait_ge(a_nT_ready, (t + u + 1) * 2)
                    nc.scalar.copy(a_nT[:, :, bass.ds((t + u) * P, P)], a_nTt[u][:]).then_inc(a_nT_copied, 1)
                    for n, width in enumerate((512, 512, TOKW - 1024)):
                        act.wait_ge(a_tok_mm, (t + u) * 3 + n + 1)
                        if n == 0:
                            act.wait_ge(rows_stored[u], t * 8)
                        nc.scalar.copy(a_tok[u][:, n * 512:n * 512 + width], bank[2 + n][:, 0:width]).then_inc(a_tok_ready, 1)

            token_pair(0)
            with act.Fori(1, NT // 2) as pair:
                token_pair(pair * 2)

            act.wait_ge(a_halo_zero, 1)
            def channel_pair(ct):
                for u in range(2):
                    for half in range(2):
                        act.wait_ge(a_channels_mm, (ct + u) * 2 + half + 1)
                        nc.scalar.copy(a_in[u][:, CONV - 1 + half * 512:CONV - 1 + half * 512 + 512],
                                            bank[2 * u + half][:, :]).then_inc(a_in_ready, 1)
                    act.wait_ge(a_conv_sum, (ct + u + 1) * CONV)
                    act.wait_ge(a_conv_stored[u], ct * 8)
                    f(a_out[u][:], a_cv[u][:], ACT.Silu).then_inc(a_conv_ready, 1)

            channel_pair(0)
            with act.Fori(1, QKV // P // 2) as pair:
                channel_pair(pair * 2)

            for b in range(4):
                act.wait_ge(keys_T, b + 1)
                half, h0 = b // 2, (b % 2) * 4
                nc.scalar.copy(keysT[:].rearrange("p (h f) n -> p f h n", f=2)[:, half, h0:h0 + 4, :],
                                    bank[b][:, :].rearrange("p (h n) -> p h n", n=P)).then_inc(keysT_ready, 1)
            for h in range(NH):
                act.wait_ge(rel_mm, h + 1)
                nc.scalar.copy(rel_rows[:, h, :], bank[4 + h % 2][:, 0:RELS]).then_inc(rel_rows_ready, 1)
            act.wait_ge(params_b, 16 * 9)
            f(neg_rate[:], a_rate[:], ACT.Exp).then_inc(rate_exp, 1)

            def norm_root(n, ap):
                act.wait_ge(mean_square, n + 1)
                f(ap, ap, ACT.Sqrt).then_inc(root, 1)

            def piece0(t):
                act.wait_ge(vector_front, t)
                for i in range(2):
                    act.wait_ge(qkv_tok, 3 * t + i + 1)
                    f(square[:, i * GW:i * GW + GW], bank[i][:, :], ACT.Square).then_inc(squares, 1)
                norm_root(norm_of(t, 0), rst)

            def piece1(t):
                act.wait_ge(tok_loaded, (t + 1) * 16)
                f(eb, tokp[:, B0:B0 + NH], ACT.Exp, scale=-1.0).then_inc(beta_exp, 1)
                act.wait_ge(x_abs, t + 1)
                f(e2, xabs, ACT.Exp, scale=-1.0).then_inc(x_exp, 1)
                act.wait_ge(x_exp, t + 1)
                f(spl, e2, ACT.Ln, bias=1.0).then_inc(softplus_tail, 1)
                act.wait_ge(gcs_ready, t + 1)
                f(eg, gcs[:, 0:NH], ACT.Exp)
                pairs = gcs[:, 16:32].rearrange("p (c q r) -> p r c q", c=2, r=2)
                for r in range(2):
                    f(glp[r * HD:r * HD + HD], pairs[r * HD:r * HD + HD, r], ACT.Exp)
                act.wait_ge(k_gap, t + 1)
                f(kd, kgap, ACT.Exp).then_inc(decays, 1)
                act.wait_ge(dec_arg, t + 1)
                f(decT, decT, ACT.Exp).then_inc(dec_exp, 1)

            def piece2(t):
                for i, (dst, b) in enumerate(((knT, 3), (nkbT, 4), (qnT, 5), (qgT, 0))):
                    act.wait_ge(heads_T, 4 * t + i + 1)
                    nc.scalar.copy(dst.rearrange("p q n -> p (q n)"), bank[b][:, :]).then_inc(heads_T_out, 1)

            def inverse_out(t, n):
                for r in range(2):
                    act.wait_ge(inv_turned, 10 * t + n + r + 1)
                    nc.scalar.copy(inv[:, 4 * r:4 * r + 4, :].rearrange("p s n -> p (s n)"),
                                        bank[(0, 5)[r]][:, :]).then_inc(inv_ready, 1)

            def piece3(t):
                act.wait_ge(qkT_ready, 2 * t + 2)
                inverse_out(t, 0)

            def level(t, l):
                for r in range(2):
                    act.wait_ge(level_x, 10 * t + 2 * (l - 1) + r + 1)
                    nc.scalar.copy(step_x[:, 4 * r:4 * r + 4, :].rearrange("p s n -> p (s n)"),
                                        bank[1 + r][:, :]).then_inc(level_x_out, 1)
                if l < LEVELS - 1:
                    inverse_out(t, 2 * l)

            def piece6(t):
                level(t, 5)
                act.wait_ge(nw_mm, t + 1)
                nc.scalar.copy(nwT.rearrange("p q n -> p (q n)"), bank[0][:, :]).then_inc(nw_out, 1)
                act.wait_ge(u_mm, t + 1)
                nc.scalar.copy(u_sb, bank[5][:, :]).then_inc(u_out, 1)

            def piece8(t):
                f(zs, tokp[:, Z0:Z0 + GW], ACT.Silu).then_inc(silu_z, 1)
                act.wait_ge(o_inter_mm, 2 * t + 2)
                for r in range(2):
                    nc.scalar.copy(o_inter.rearrange("p (q r d) -> p r q d", r=2, d=HD)[:, r],
                                        bank[3 + r][:, 0:256].rearrange("p (q d) -> p q d", d=HD)).then_inc(o_inter_out, 1)
                act.wait_ge(o_sum, t + 1)
                f(o_sq, o_sb, ACT.Square).then_inc(o_squares, 1)
                norm_root(norm_of(t, 1), o_rs)
                act.wait_ge(o_T, t + 1)
                nc.scalar.copy(mixT[:, 0:4, :].rearrange("p s n -> p (s n)"), bank[0][:, :]).then_inc(mix_ready, 1)

            def piece9(t):
                f(s_sq, tokp[:, SQ0:SV0], ACT.Square).then_inc(s_squares, 1)
                norm_root(norm_of(t, 2), s_rs)
                act.wait_ge(s_T, t + 1)
                f(sqT.rearrange("p q n -> p (q n)"), bank[1][:, :], ACT.Copy, scale=q_gain[:, 0:1]).then_inc(s_T_out, 1)
                act.wait_ge(window_moved, t + 1)
                f(kwin[:, CHUNK:WIN], bank[2][:, 0:P], ACT.Copy, scale=k_gain[:, 0:1]).then_inc(s_T_out, 1)
                act.wait_ge(s_max, t + 1)
                for h in range(NH):
                    f(probs[:, h, CHUNK:256], probs[:, h, CHUNK:256], ACT.Exp, bias=s_nm[:, h:h + 1],
                      accum_out=s_den[:, h:h + 1])
                f(s_es, s_gap, ACT.Exp).then_inc(s_exp, 1)

            def piece10(t):
                for b in range(4):
                    act.wait_ge(probs_T, 4 * t + b + 1)
                    nc.scalar.copy(probsT[:, 4 * b:4 * b + 4, :].rearrange("p s n -> p (s n)"),
                                        bank[1 + b][:, :]).then_inc(probsT_ready, 1)

            def piece11(t):
                act.wait_ge(av_mm, t + 1)
                nc.scalar.copy(mixT[:, 4:8, :].rearrange("p s n -> p (s n)"), bank[5][:, :]).then_inc(mix_ready, 1)

            def piece12(t):
                act.wait_ge(h1_ready, 2 * t + 2)
                f(h_junk, h1, ACT.Square, accum_out=h_ss).then_inc(row_squares, 1)
                norm_root(norm_of(t, 3), h_rs)
                for i in range(2):
                    act.wait_ge(n2_T, 2 * t + i + 1)
                    nc.scalar.copy(n2T[:, 4 * i:4 * i + 4, :].rearrange("p s n -> p (s n)"), bank[2 + i][:, :]).then_inc(n2T_ready, 1)

            def query(t, i):
                act.wait_ge(query_mm, NQ * t + i + 1)
                nc.scalar.copy(qr, bank[4][:, 0:QCOL]).then_inc(qr_ready, 1)
                act.wait_ge(qr_T, NQ * t + i + 1)
                nc.scalar.copy(qrT.rearrange("p s n -> p (s n)"), bank[5][:, 0:QCOL]).then_inc(qrT_ready, 1)
                act.wait_ge(score_mm, NQ * t + i + 1)
                nc.scalar.copy(scores[:, 2 * i:2 * i + 2, :].rearrange("p s n -> p (s n)"),
                                    bank[i % 2][:, 0:QCOL]).then_inc(scores_ready, 1)

            def piece_gate(t):
                act.wait_ge(gate_arg, t + 1)
                f(gate_new[:], gate_new[:], ACT.Exp).then_inc(gate_exp, 1)

            pieces = [piece0, piece1, lambda t: (piece2(t), piece3(t)),
                      lambda t: (level(t, 1), level(t, 2)), lambda t: (level(t, 3), level(t, 4)), piece6,
                      lambda t: None, piece8, piece9, lambda t: (piece10(t), piece11(t)), piece12,
                      lambda t: (query(t, 0), query(t, 1)), lambda t: (query(t, 2), query(t, 3)),
                      lambda t: (query(t, 4), query(t, 5)), lambda t: (query(t, 6), query(t, 7), piece_gate(t)),
                      lambda t: None]
            assert len(pieces) == NG

            def experts(t, g):
                act.wait_ge(u_used, t * SLOTS + g * G + G)
                f(gel[:, g * G:g * G + G], hid[:, g * G:g * G + G], ACT.Gelu).then_inc(gelu, 1)
                act.wait_ge(weights_ready, t * NG + g + 1)
                for j in range(G):
                    if not (isinstance(t, int) and t == 0 and g == 0):
                        act.wait_ge(v_used, t * SLOTS + (g - 1) * G + j + 1)
                    f(diag[:, j, :], ident, ACT.Copy, scale=act_w[:, g * G + j:g * G + j + 1]).then_inc(diag_ready, 1)

            for i in range(NG):
                pieces[i](0)
            for g in range(NG):
                experts(0, g)
                pieces[g](1)
            with act.Fori(2, NT) as t:
                for g in range(NG):
                    experts(t - 1, g)
                    pieces[g](t)
            for g in range(NG):
                experts(NT - 1, g)

            with act.Fori(0, NT // 2) as pair:
                t = pair * 2
                for u in range(2):
                    k = t + u
                    act.wait_ge(rows_in[u], 8 * NT + t * 16 + 32)
                    f(c_junk[:], c_h[u][:], ACT.Square, accum_out=c_ss).then_inc(row_squares, 1)
                    act.wait_ge(mean_square, 5 * NT + k + 1)
                    f(c_rs, c_rs, ACT.Sqrt).then_inc(root, 1)
                    for i in range(2):
                        act.wait_ge(n2_T, 2 * NT + 2 * k + i + 1)
                        nc.scalar.copy(c_nT[:, 4 * i:4 * i + 4, :].rearrange("p s n -> p (s n)"), bank[i][:, :]).then_inc(n2T_ready, 1)
                    for i in range(2):
                        act.wait_ge(h1_mm, 2 * NT + 2 * k + i + 1)
                        f(c_e[:, i * 512:i * 512 + 512], bank[3 + i][:, :], ACT.Sigmoid).then_inc(c_gate, 1)

        @block.tensor
        def _(pe):
            def mm(out_, lhsT, rhs, start=True, stop=True, **kw):
                return nc.tensor.matmul(out_, lhsT, rhs, start=start, stop=stop, **kw)

            def turn(out_, in_):
                return nc.tensor.transpose(out_, in_, ident)

            pe.wait_ge(consts_loaded, 16)
            pe.wait_ge(a_w_loaded, 64)
            def token_pair(t):
                for u in range(2):
                    pe.wait_ge(a_n_ready, t + u + 1)
                    pe.wait_ge(a_nT_ready, (t + u) * 2)
                    for c in range(DC):
                        last = turn(bank[c // 4][:, (c % 4) * P:(c % 4) * P + P], a_n[u][:, c * P:c * P + P])
                        if c % 4 == 3:
                            last.then_inc(a_turned, 1)
                    pe.wait_ge(a_nT_ready, (t + u + 1) * 2)
                    for n, width in enumerate((512, 512, TOKW - 1024)):
                        pe.wait_ge(a_tok_ready, (t + u) * 3)
                        for c in range(DC):
                            last = mm(bank[2 + n][:, 0:width], a_nTt[u][:, c, :], a_w[:, c, n * 512:n * 512 + width],
                                      c == 0, c == DC - 1)
                        last.then_inc(a_tok_mm, 1)

            token_pair(0)
            with pe.Fori(1, NT // 2) as pair:
                token_pair(pair * 2)

            pe.wait_ge(a_nT_copied, NT)
            pe.wait_ge(a_tok_ready, 3 * NT)

            def channels(ct, u):
                pe.wait_ge(wq_loaded[u], ct * 8 + 16)
                if not isinstance(ct, int):
                    pe.wait_ge(a_in_ready, (ct + u) * 2 - 2)
                for half in range(2):
                    for c in range(DC):
                        last = mm(bank[2 * u + half][:, :], a_wc[u][:, c, :], a_nT[:, c, half * 512:half * 512 + 512],
                                  c == 0, c == DC - 1)
                    last.then_inc(a_channels_mm, 1)

            for u in range(2):
                channels(0, u)
            with pe.Fori(1, QKV // P // 2) as pair:
                ct = pair * 2
                for u in range(2):
                    channels(ct, u)

            pe.wait_ge(a_in_ready, QKV // P * 2)
            pe.wait_ge(keys_loaded, 16)
            for i in range(NHH):
                last = turn(bank[i // 4][:, (i % 4) * P:(i % 4) * P + P], keys_in[:, i, :])
                if i % 4 == 3:
                    last.then_inc(keys_T, 1)
            pe.wait_ge(params_b, 16 * 9)
            for h in range(NH):
                if h >= 2:
                    pe.wait_ge(rel_rows_ready, h - 1)
                mm(bank[4 + h % 2][:, 0:RELS], rel_sb[:, h:h + 1].broadcast_to([REL_BUCKETS, P]),
                        cst[0:REL_BUCKETS, C_REL:C_REL + RELS]).then_inc(rel_mm, 1)
            pe.wait_ge(keysT_ready, 4)
            pe.wait_ge(rel_rows_ready, NH)

            def piece0(t):
                pe.wait_ge(vector_front, t)
                pe.wait_ge(qkv_loaded, (t + 1) * 16)
                for c in range(QKV // P):
                    last = turn(bank[c // 4][:, (c % 4) * P:(c % 4) * P + P], qkv_in[:, c, :])
                    if c % 4 == 3:
                        last.then_inc(qkv_tok, 1)

            def piece1(t):
                pe.wait_ge(g_ready, t + 1)
                for i, at in enumerate((C_TRIL, C_BLOCK, C_CH0, C_CH1)):
                    last = mm(bank[3][:, 8 * i:8 * i + 8], cst[:, at:at + P], gl)
                last.then_inc(cumsum, 1)
                for r in range(2):
                    pe.wait_ge(gdiag_ready, 2 * t + r + 1)
                    mm(bank[4 + r][:, :], cst[:, C_ONES:C_ONES + P],
                            gdiag[:, 4 * r:4 * r + 4, :].rearrange("p s n -> p (s n)")).then_inc(gc_rows, 1)

            def piece2(t):
                for i, (src, b) in enumerate(((kn, 3), (nkb, 4), (qn, 5), (qg, 0))):
                    pe.wait_ge(scaled, 7 * t + i + 1)
                    for q in range(4):
                        last = turn(bank[b][:, q * P:q * P + P], src[:, q * P:q * P + P])
                    last.then_inc(heads_T, 1)

            def turn_inverse(t, n):
                for r in range(2):
                    pe.wait_ge(invT_ready, 12 * t + n + r + 1)
                    for q in range(4):
                        last = turn(bank[(0, 5)[r]][:, q * P:q * P + P], invT[:, 4 * r + q, :])
                    last.then_inc(inv_turned, 1)

            def piece3(t):
                pe.wait_ge(scaled, 7 * t + 7)
                pe.wait_ge(heads_T_out, 4 * t + 2)
                for r in range(2):
                    for q in range(4):
                        last = mm(bank[1 + r][:, q * P:q * P + P], knT[r * HD:r * HD + HD, q, :], nkbT[r * HD:r * HD + HD, q, :])
                    last.then_inc(kk_mm, 1)
                pe.wait_ge(heads_T_out, 4 * t + 3)
                for r in range(2):
                    for q in range(4):
                        last = mm(bank[3 + r][:, q * P:q * P + P], knT[r * HD:r * HD + HD, q, :], qnT[r * HD:r * HD + HD, q, :])
                    last.then_inc(qk_mm, 1)
                pe.wait_ge(heads_T_out, 4 * t + 4)
                turn_inverse(t, 0)

            def level(t, l):
                n = 10 * t + 2 * (l - 1)
                for r in range(2):
                    pe.wait_ge(inv_ready, n + r + 1)
                    for q in range(4):
                        last = mm(bank[1 + r][:, q * P:q * P + P], amT[:, 4 * r + q, :], inv[:, 4 * r + q, :])
                    last.then_inc(level_x, 1)
                for r in range(2):
                    pe.wait_ge(level_x_out, n + r + 1)
                    for q in range(4):
                        last = mm(bank[3 + r][:, q * P:q * P + P], step_x[:, 4 * r + q, :], invT[:, 4 * r + q, :])
                    last.then_inc(level_p, 1)
                if l < LEVELS - 1:
                    turn_inverse(t, 2 * l)

            def piece6(t):
                level(t, 5)
                pe.wait_ge(invT_ready, 12 * t + 12)
                for q in range(4):
                    for r in range(2):
                        h, s = 2 * q + r, 4 * r + q
                        last = mm(bank[0][r * HD:r * HD + HD, q * P:q * P + P], nkbg[:, h * HD:h * HD + HD], invT[:, s, :])
                last.then_inc(nw_mm, 1)
                for h in range(NH):
                    last = mm(bank[5][:, h * HD:h * HD + HD], invT[:, 4 * (h % 2) + h // 2, :], vb[:, h * HD:h * HD + HD])
                last.then_inc(u_mm, 1)

            def piece7(t, c):
                rows = slice(c * CHUNK, c * CHUNK + CHUNK)
                pe.wait_ge(nw_out, t + 1)
                pe.sem_inc(wait_carrier)
                pe.wait_ge(state_ready, 2 * t + c + 1)
                pe.sem_inc(wait_carrier)
                for r in range(2):
                    chans = slice(r * HD, r * HD + HD)
                    for q in range(4):
                        last = mm(bank[1 + r][rows, q * HD:q * HD + HD], nwT[chans, q, rows], state[chans, q, :])
                last.then_inc(ws_mm, 1)
                for r in range(2):
                    chans = slice(r * HD, r * HD + HD)
                    for q in range(4):
                        last = mm(bank[3 + r][rows, q * HD:q * HD + HD], qgT[chans, q, rows], state[chans, q, :])
                last.then_inc(o_inter_mm, 1)
                pe.wait_ge(v_new_ready, 4 * t + 2 * c + 2)
                pe.sem_inc(wait_carrier)
                for h in range(NH):
                    r, q = h % 2, h // 2
                    last = mm(bank[0][r * HD:r * HD + HD, q * HD:q * HD + HD], kdec[rows, h * HD:h * HD + HD],
                              v_new[rows, h * HD:h * HD + HD])
                last.then_inc(kv_mm, 1)

            def piece8(t):
                for h in range(NH):
                    last = mm(bank[5][:, h * HD:h * HD + HD], qkT[:, 4 * (h % 2) + h // 2, :], v_new[:, h * HD:h * HD + HD])
                last.then_inc(o_intra_mm, 1)
                pe.wait_ge(state_ready, 2 * t + 3)
                pe.wait_ge(o_normed, t + 1)
                for q in range(4):
                    last = turn(bank[0][:, q * P:q * P + P], o_sb[:, q * P:q * P + P])
                last.then_inc(o_T, 1)

            def piece9(t):
                pe.wait_ge(s_normed, 2 * t + 2)
                for q in range(4):
                    turn(bank[1][:, q * P:q * P + P], s_n[:, q * P:q * P + P])
                turn(bank[2][:, 0:P], s_n[:, GW:GW + P]).then_inc(s_T, 1)
                pe.wait_ge(s_T_out, 2 * t + 2)
                pe.wait_ge(mix_ready, 2 * t + 1)
                for h in range(NH):
                    kv, g = h // 4, h % 4
                    chans = slice(kv * HD, kv * HD + HD)
                    last = mm(bank[bias_banks[h // 2]][:, (h % 2) * WIN:(h % 2) * WIN + WIN], sqT[chans, g, :],
                              kwin[chans, :])
                    if h % 2:
                        last.then_inc(logits_mm, 1)

            def piece10(t):
                pe.wait_ge(probs_ready, t + 1)
                for i in range(16):
                    last = turn(bank[1 + i // 4][:, (i % 4) * P:(i % 4) * P + P], probs[:, i // 2, (i % 2) * P:(i % 2) * P + P])
                    if i % 4 == 3:
                        last.then_inc(probs_T, 1)

            def piece11(t):
                pe.wait_ge(probsT_ready, 4 * t + 4)
                for h in range(NH):
                    kv = h // 4
                    to = bank[5][(h % 2) * HD:(h % 2) * HD + HD, (h // 2) * P:(h // 2) * P + P]
                    mm(to, vprev[:, kv * HD:kv * HD + HD], probsT[:, 2 * h, :], True, False)
                    last = mm(to, vcur[:, kv * HD:kv * HD + HD], probsT[:, 2 * h + 1, :], False, True)
                last.then_inc(av_mm, 1)
                pe.wait_ge(mix_ready, 2 * t + 2)
                pe.wait_ge(w_out_loaded, 32)
                project_out(0)

            def project_out(n):
                for c in range(DC):
                    last = mm(bank[n][:, :], mixT[:, c, :], w_out_sb[:, c, n * 512:n * 512 + 512], c == 0, c == DC - 1)
                last.then_inc(h1_mm, 1)

            def piece12(t):
                pe.wait_ge(xb_ready, t + 1)
                for c in range(DC):
                    last = turn(bank[2 + c // 4][:, (c % 4) * P:(c % 4) * P + P], xb_new[:, c * P:c * P + P])
                    if c % 4 == 3:
                        last.then_inc(n2_T, 1)
                pe.wait_ge(n2T_ready, 2 * t + 2)

            def query(t, i):
                pe.wait_ge(wq_loaded[i % 2], 8 * (QKV // P) + 16 * (NQ // 2) * t + 16 * (i // 2) + 16)
                for c in range(DC):
                    last = mm(bank[4][:, 0:QCOL], n2T[:, c, :], wq[i % 2][:, c, :], c == 0, c == DC - 1)
                last.then_inc(query_mm, 1)
                pe.wait_ge(qr_ready, NQ * t + i + 1)
                for s in range(2):
                    last = turn(bank[5][:, s * P:s * P + P], qr[:, s * P:s * P + P])
                last.then_inc(qr_T, 1)
                pe.wait_ge(qrT_ready, NQ * t + i + 1)
                pe.wait_ge(scores_ready, NQ * t + max(i - 1, 0))
                for s in range(2):
                    last = mm(bank[i % 2][:, s * P:s * P + P], qrT[:, s, :], keysT[:, 2 * i + s, :])
                last.then_inc(score_mm, 1)

            pieces = [piece0, piece1, lambda t: (piece2(t), piece3(t)),
                      lambda t: (level(t, 1), level(t, 2)), lambda t: (level(t, 3), level(t, 4)), piece6,
                      lambda t: (piece7(t, 0), piece7(t, 1)), piece8, piece9, lambda t: (piece10(t), piece11(t)),
                      lambda t: (project_out(1), piece12(t)),
                      lambda t: (query(t, 0), query(t, 1)), lambda t: (query(t, 2), query(t, 3)),
                      lambda t: (query(t, 4), query(t, 5)), lambda t: (query(t, 6), query(t, 7)), lambda t: None]

            def experts(t, g):
                if g == 0:
                    pe.wait_ge(h2_ready, t * 2)
                for j in range(G):
                    pe.wait_ge(v_landed[j], (t * NG + g + 1) * 16)
                    pe.wait_ge(diag_ready, t * SLOTS + g * G + j + 1)
                    for n in range(2):
                        last = mm(acc[:, n * 512:n * 512 + 512], diag[:, j, :], v_ring[:, j, n * 512:n * 512 + 512],
                                  g == 0 and j == 0, g == NG - 1 and j == G - 1)
                    last.then_inc(v_used, 1)

            def tile(t):
                for g in range(NG):
                    if g:
                        experts(t - 1, g - 1)
                    pieces[g](t)
                experts(t - 1, NG - 1)

            for i in range(NG):
                pieces[i](0)
            tile(1)
            with pe.Fori(2, NT) as t:
                tile(t)
            for g in range(NG):
                experts(NT - 1, g)

            pe.wait_ge(c_w_loaded, 48)
            def gate_pair(t):
                for u in range(2):
                    k = t + u
                    pe.wait_ge(rows_in[u], 8 * NT + t * 16 + 32)
                    pe.wait_ge(c_out_ready, k)
                    for c in range(PLE // P):
                        last = turn(bank[2][:, c * P:c * P + P], c_p[u][:, c * P:c * P + P])
                    last.then_inc(c_pT_turned, 1)
                    pe.wait_ge(xb_ready, NT + k + 1)
                    for c in range(DC):
                        last = turn(bank[c // 4][:, (c % 4) * P:(c % 4) * P + P], c_n[:, c * P:c * P + P])
                        if c % 4 == 3:
                            last.then_inc(n2_T, 1)
                    pe.wait_ge(c_pT_ready, k + 1)
                    for n in range(2):
                        for c in range(PLE // P):
                            last = mm(acc[:, n * 512:n * 512 + 512], c_pT[:, c, :], wp_sb[:, c, n * 512:n * 512 + 512],
                                      c == 0, c == PLE // P - 1)
                    last.then_inc(c_proj_mm, 1)
                    pe.wait_ge(n2T_ready, 2 * NT + 2 * k + 2)
                    for n in range(2):
                        for c in range(DC):
                            last = mm(bank[3 + n][:, :], c_nT[:, c, :], wg_sb[:, c, n * 512:n * 512 + 512],
                                      c == 0, c == DC - 1)
                        last.then_inc(h1_mm, 1)

            gate_pair(0)
            with pe.Fori(1, NT // 2) as pair:
                gate_pair(pair * 2)

        @block.vector
        def _(dve):
            v = nc.vector
            counted = [0]

            def steps(t):
                counted[0] += 1
                return t * V_STEPS + counted[0]

            def mean_to_ms(out_, in_, n):
                return v.tensor_scalar(out_, in_, 1.0 / n, EPS, ALU.mult, ALU.add)

            dve.wait_ge(params_a, 16 * (CONV + 1))
            for u in range(2):
                last = v.memset(a_in[u][:, 0:CONV - 1], 0.0)
            last.then_inc(a_halo_zero, 1)
            with dve.Fori(0, NT // 2) as pair:
                t = pair * 2
                for u in range(2):
                    dve.wait_ge(row_squares, t + u + 1)
                    mean_to_ms(a_rs[:, u:u + 1], a_ss[:, u:u + 1], D).then_inc(mean_square, 1)
                    dve.wait_ge(root, t + u + 1)
                    v.reciprocal(a_rs[:, u:u + 1], a_rs[:, u:u + 1]).then_inc(inverse_root, 1)
                    dve.wait_ge(inverse_root, t + u + 1)
                    v.tensor_scalar(a_n[u][:], a_x[u][:], a_rs[:, u:u + 1], None, ALU.mult).then_inc(a_n_ready, 1)
                    for i in range(2):
                        dve.wait_ge(a_turned, (t + u) * 2 + i + 1)
                        v.tensor_tensor(a_nTt[u][:, 4 * i:4 * i + 4, :], bank[i][:, :].rearrange("p (c n) -> p c n", n=P),
                                             per_head(g_mix_c[:, 4 * i:4 * i + 4], 4, P), ALU.mult).then_inc(a_nT_ready, 1)
            dve.wait_ge(params_a, 16 * (CONV + 1))
            with dve.Fori(0, QKV // P // 2) as pair:
                ct = pair * 2
                for u in range(2):
                    dve.wait_ge(a_in_ready, (ct + u + 1) * 2)
                    for k in range(CONV):
                        tap = conv_c[:, k, bass.ds(ct + u, 1)]
                        if k == 0:
                            ins = v.tensor_scalar(a_cv[u][:], a_in[u][:, k:k + SEQ], tap, None, ALU.mult)
                        else:
                            dve.wait_ge(a_conv_sum, (ct + u) * CONV + k)
                            ins = v.scalar_tensor_tensor(a_cv[u][:], a_in[u][:, k:k + SEQ], tap, a_cv[u][:], ALU.mult, ALU.add)
                        ins.then_inc(a_conv_sum, 1)

            dve.wait_ge(a_conv_ready, QKV // P)
            for u in range(2):
                dve.wait_ge(a_conv_stored[u], 16 * QKV // P // 2)
                dve.wait_ge(rows_stored[u], 16 * NT // 2)
            v.memset(kwin[:], 0.0)
            v.memset(vcur[:], 0.0)
            v.memset(v_new, 0.0)
            v.memset(state[:], 0.0).then_inc(state_ready, 1)
            dve.wait_ge(rate_exp, 1)
            v.tensor_scalar(neg_rate[:], neg_rate[:], -1.0, None, ALU.mult).then_inc(rate_ready, 1)
            dve.wait_ge(rate_ready, 1)
            dve.wait_ge(bias_loaded, 16)
            v.tensor_tensor(bias_t[:], bias_t[:], cst[:, C_WIN:C_WIN + WIN].unsqueeze(1).broadcast_to([P, NH, WIN]),
                                 ALU.add).then_inc(bias_ready, 1)
            dve.wait_ge(bias_ready, 1)
            dve.wait_ge(state_ready, 1)
            dve.wait_ge(w_out_loaded, 32)

            def gc_of(r, width=P):
                return gcs[:, 0:NH].rearrange("p (q r) -> p r q", r=2)[:, r].unsqueeze(2).broadcast_to([P, 4, width])

            def piece0(t):
                dve.wait_ge(vector_front, t)
                dve.wait_ge(h1_stored, 16 * t)
                dve.wait_ge(squares, 2 * t + 2)
                v.reduce_sum(ssq, square.rearrange("p (h d) -> p h d", d=HD), AX.X).then_inc(vector_step, 1)
                dve.wait_ge(vector_step, steps(t))
                v.tensor_scalar(rst, ssq, EPS, None, ALU.add).then_inc(mean_square, 1)
                dve.wait_ge(root, norm_of(t, 0) + 1)
                v.reciprocal(rst, rst).then_inc(vector_step, 1)
                dve.wait_ge(vector_step, steps(t))
                v.tensor_scalar(rst[:, 0:NH], rst[:, 0:NH], HD ** -0.5, None, ALU.mult).then_inc(vector_step, 1)
                dve.wait_ge(vector_step, steps(t))

            def piece1(t):
                dve.wait_ge(tok_loaded, (t + 1) * 16)
                v.tensor_tensor(xa, tokp[:, A0:A0 + NH], dt_row[:], ALU.add).then_inc(vector_step, 1)
                dve.wait_ge(vector_step, steps(t))
                v.scalar_tensor_tensor(xabs, xa, -1.0, xa, ALU.mult, ALU.max).then_inc(x_abs, 1)
                dve.wait_ge(beta_exp, t + 1)
                v.tensor_scalar(eb, eb, 1.0, None, ALU.add).then_inc(vector_step, 1)
                dve.wait_ge(vector_step, steps(t))
                v.reciprocal(beta, eb).then_inc(vector_step, 1)
                dve.wait_ge(vector_step, steps(t))
                v.tensor_scalar(nbeta, beta, -1.0, None, ALU.mult).then_inc(vector_step, 1)
                dve.wait_ge(vector_step, steps(t))
                dve.wait_ge(softplus_tail, t + 1)
                v.scalar_tensor_tensor(gl, xa, 0.0, spl, ALU.max, ALU.add).then_inc(vector_step, 1)
                dve.wait_ge(vector_step, steps(t))
                v.tensor_tensor(gl, gl, neg_rate[:], ALU.mult).then_inc(g_ready, 1)
                dve.wait_ge(cumsum, t + 1)
                v.tensor_copy(gcs, bank[3][:, 0:32]).then_inc(gcs_ready, 1)
                dve.wait_ge(gcs_ready, t + 1)
                v.tensor_tensor(kgap, gcs[:, NH:2 * NH], gcs[:, 0:NH], ALU.subtract).then_inc(k_gap, 1)
                for r in range(2):
                    v.tensor_tensor(gdiag[:, 4 * r:4 * r + 4, :], ident.unsqueeze(1).broadcast_to([P, 4, P]), gc_of(r),
                                         ALU.mult).then_inc(gdiag_ready, 1)
                for r in range(2):
                    dve.wait_ge(gc_rows, 2 * t + r + 1)
                    last = v.tensor_tensor(decT[:, 4 * r:4 * r + 4, :], bank[4 + r][:, :].rearrange("p (s n) -> p s n", n=P),
                                           gc_of(r), ALU.subtract)
                last.then_inc(vector_step, 1)
                dve.wait_ge(vector_step, steps(t))
                v.tensor_scalar(decT, decT, 0.0, None, ALU.min).then_inc(dec_arg, 1)
                dve.wait_ge(dec_exp, t + 1)
                v.tensor_tensor(decT, decT, cst[:, C_TRIL:C_TRIL + P].unsqueeze(1).broadcast_to([P, 8, P]), ALU.mult).then_inc(vector_step, 1)
                dve.wait_ge(vector_step, steps(t))

            def piece2(t):
                dve.wait_ge(qkv_tok, 3 * t + 3)
                dve.wait_ge(decays, t + 1)
                n = 7 * t
                for i, (dst, src, factor, need) in enumerate((
                        (kn, bank[1][:, :], rst[:, NH:2 * NH], 0), (nkb, kn, nbeta, 1), (qn, bank[0][:, :], rst[:, 0:NH], 0),
                        (qg, qn, eg, 3), (nkbg, nkb, eg, 2), (vb, bank[2][:, :], beta, 0), (kdec, kn, kd, 1))):
                    if need:
                        dve.wait_ge(scaled, n + need)
                    v.tensor_tensor(heads(dst), heads(src), per_head(factor), ALU.mult).then_inc(scaled, 1)

            def level_mask(l):
                return cst[:, C_LEVEL + l * P:C_LEVEL + l * P + P].bitcast(U32).unsqueeze(1).broadcast_to([P, 4, P])

            def piece3(t):
                for r in range(2):
                    dve.wait_ge(kk_mm, 2 * t + r + 1)
                    last = v.tensor_tensor(amT[:, 4 * r:4 * r + 4, :], bank[1 + r][:, :].rearrange("p (s n) -> p s n", n=P),
                                           decT[:, 4 * r:4 * r + 4, :], ALU.mult)
                dve.wait_ge(heads_T, 4 * t + 4)
                v.tensor_copy(invT, ident.unsqueeze(1).broadcast_to([P, 8, P])).then_inc(vector_step, 1)
                dve.wait_ge(vector_step, steps(t))
                dve.sem_inc(wait_carrier)
                for r in range(2):
                    v.copy_predicated(invT[:, 4 * r:4 * r + 4, :], level_mask(0), amT[:, 4 * r:4 * r + 4, :]).then_inc(invT_ready, 1)
                for r in range(2):
                    dve.wait_ge(qk_mm, 2 * t + r + 1)
                    v.tensor_tensor(qkT[:, 4 * r:4 * r + 4, :], bank[3 + r][:, :].rearrange("p (s n) -> p s n", n=P),
                                         decT[:, 4 * r:4 * r + 4, :], ALU.mult).then_inc(qkT_ready, 1)

            def level(t, l):
                for r in range(2):
                    dve.wait_ge(level_p, 10 * t + 2 * (l - 1) + r + 1)
                    dve.sem_inc(wait_carrier)
                    v.copy_predicated(invT[:, 4 * r:4 * r + 4, :], level_mask(l),
                                           bank[3 + r][:, :].rearrange("p (s n) -> p s n", n=P)).then_inc(invT_ready, 1)

            def piece7(t, c):
                rows = slice(c * CHUNK, c * CHUNK + CHUNK)
                dve.wait_ge(u_out, t + 1)
                dve.wait_ge(ws_mm, 2 * t + c + 1)
                by_r = lambda ap: ap[rows, :].rearrange("p (q r d) -> p r q d", r=2, d=HD)
                for r in range(2):
                    v.tensor_tensor(by_r(v_new)[:, r], by_r(u_sb)[:, r],
                                         bank[1 + r][rows, 0:256].rearrange("p (q d) -> p q d", d=HD), ALU.add).then_inc(v_new_ready, 1)
                dve.wait_ge(kv_mm, 2 * t + c + 1)
                v.tensor_tensor(state[:], state[:], per_head(glp[:, c, :], 4), ALU.mult).then_inc(vector_step, 1)
                dve.wait_ge(vector_step, steps(t))
                v.tensor_tensor(state[:], state[:], bank[0][:, 0:256].rearrange("p (q d) -> p q d", d=HD), ALU.add).then_inc(state_ready, 1)

            def piece8(t):
                dve.wait_ge(silu_z, t + 1)
                v.tensor_tensor(heads(zs), heads(zs), norm_g[:].unsqueeze(1).broadcast_to([P, NH, HD]), ALU.mult).then_inc(vector_step, 1)
                dve.wait_ge(vector_step, steps(t))
                dve.wait_ge(o_inter_out, 2 * t + 2)
                dve.wait_ge(o_intra_mm, t + 1)
                v.tensor_tensor(o_sb, o_inter, bank[5][:, :], ALU.add).then_inc(o_sum, 1)
                dve.wait_ge(o_squares, t + 1)
                v.reduce_sum(o_ss, heads(o_sq), AX.X).then_inc(vector_step, 1)
                dve.wait_ge(vector_step, steps(t))
                mean_to_ms(o_rs, o_ss, HD).then_inc(mean_square, 1)
                dve.wait_ge(root, norm_of(t, 1) + 1)
                v.reciprocal(o_rs, o_rs).then_inc(vector_step, 1)
                dve.wait_ge(vector_step, steps(t))
                v.tensor_tensor(heads(o_sb), heads(o_sb), per_head(o_rs), ALU.mult).then_inc(vector_step, 1)
                dve.wait_ge(vector_step, steps(t))
                v.tensor_tensor(o_sb, o_sb, zs, ALU.mult).then_inc(o_normed, 1)

            def piece9(t):
                v.tensor_copy(kwin[:, 0:CHUNK], kwin[:, P:WIN]).then_inc(vector_step, 1)
                dve.wait_ge(vector_step, steps(t))
                v.tensor_copy(vprev[:], vcur[:]).then_inc(vector_step, 1)
                dve.wait_ge(vector_step, steps(t))
                v.tensor_copy(vcur[:], tokp[:, SV0:SV0 + P]).then_inc(window_moved, 1)
                dve.wait_ge(s_squares, t + 1)
                v.reduce_sum(s_ss, heads(s_sq, 10), AX.X).then_inc(vector_step, 1)
                dve.wait_ge(vector_step, steps(t))
                mean_to_ms(s_rs, s_ss, HD).then_inc(mean_square, 1)
                dve.wait_ge(root, norm_of(t, 2) + 1)
                v.reciprocal(s_rs, s_rs).then_inc(vector_step, 1)
                dve.wait_ge(vector_step, steps(t))
                v.tensor_scalar(s_rs[:, 0:NH], s_rs[:, 0:NH], HD ** -0.5, None, ALU.mult).then_inc(vector_step, 1)
                dve.wait_ge(vector_step, steps(t))
                v.tensor_tensor(s_n[:, 0:GW].rearrange("p (g k d) -> p k g d", k=NKV, d=HD),
                                     tokp[:, SQ0:SK0].rearrange("p (k g d) -> p k g d", k=NKV, d=HD),
                                     s_rs[:, 0:NH].rearrange("p (k g) -> p k g", k=NKV).unsqueeze(3).broadcast_to([P, NKV, 4, HD]),
                                     ALU.mult).then_inc(s_normed, 1)
                v.tensor_tensor(heads(s_n[:, GW:GW + P], 2), heads(tokp[:, SK0:SV0], 2), per_head(s_rs[:, NH:10], 2),
                                     ALU.mult).then_inc(s_normed, 1)
                v.memset(probs[:, :, 0:CHUNK], 0.0)
                for b in range(4):
                    dve.wait_ge(logits_mm, 4 * t + b + 1)
                    last = v.tensor_tensor(probs[:, 2 * b:2 * b + 2, CHUNK:256],
                                           bank[bias_banks[b]][:, 0:2 * WIN].rearrange("p (h w) -> p h w", h=2),
                                           bias_t[:, 2 * b:2 * b + 2, :], ALU.add)
                last.then_inc(vector_step, 1)
                dve.wait_ge(vector_step, steps(t))
                if isinstance(t, int) and t == 0:
                    last = v.memset(probs[:, :, CHUNK:2 * CHUNK], MASKED)
                else:
                    last = v.tensor_scalar(s_gap, sinks[:], 0.0, None, ALU.add)
                last.then_inc(vector_step, 1)
                dve.wait_ge(vector_step, steps(t))
                v.tensor_reduce(s_m, probs[:, :, CHUNK:256], AX.X, ALU.max).then_inc(vector_step, 1)
                dve.wait_ge(vector_step, steps(t))
                v.tensor_tensor(s_m, s_m, sinks[:], ALU.max).then_inc(vector_step, 1)
                dve.wait_ge(vector_step, steps(t))
                v.tensor_scalar(s_nm, s_m, -1.0, None, ALU.mult).then_inc(vector_step, 1)
                dve.wait_ge(vector_step, steps(t))
                v.tensor_tensor(s_gap, sinks[:], s_nm, ALU.add).then_inc(s_max, 1)

            def piece10(t):
                dve.wait_ge(s_exp, t + 1)
                v.tensor_tensor(s_den, s_den, s_es, ALU.add).then_inc(vector_step, 1)
                dve.wait_ge(vector_step, steps(t))
                v.reciprocal(s_den, s_den).then_inc(vector_step, 1)
                dve.wait_ge(vector_step, steps(t))
                v.tensor_tensor(probs[:, :, CHUNK:256], probs[:, :, CHUNK:256], per_head(s_den, NH, WIN), ALU.mult).then_inc(probs_ready, 1)

            def residual(t, n):
                dve.wait_ge(x_loaded, (t + 1) * 16)
                dve.wait_ge(h1_mm, 2 * t + n + 1)
                v.tensor_tensor(h1[:, n * 512:n * 512 + 512], x_t[:, n * 512:n * 512 + 512], bank[n][:, :],
                                ALU.add).then_inc(h1_ready, 1)

            def piece12(t):
                dve.wait_ge(row_squares, NT + t + 1)
                mean_to_ms(h_rs, h_ss, D).then_inc(mean_square, 1)
                dve.wait_ge(root, norm_of(t, 3) + 1)
                v.reciprocal(h_rs, h_rs).then_inc(vector_step, 1)
                dve.wait_ge(vector_step, steps(t))
                if not isinstance(t, int) or t >= 2:
                    dve.wait_ge(h2_stored, (t - 1) * 16)
                v.scalar_tensor_tensor(xb_new[:], h1, h_rs, g_ffn_b[:], ALU.mult, ALU.mult).then_inc(xb_ready, 1)

            def top16(t, values, tops, indices):
                first = slice(0, 8)
                second = slice(8, 16)
                for row, top, _ in zip(values, tops, indices):
                    last = v.max(top[:, first], row)
                last.then_inc(vector_step, 1)
                dve.wait_ge(vector_step, steps(t))
                dve.sem_inc(wait_carrier)
                for row, top, index in zip(values, tops, indices):
                    last = v.max_index(index[:, first], top[:, first], row)
                last.then_inc(vector_step, 1)
                dve.wait_ge(vector_step, steps(t))
                dve.sem_inc(wait_carrier)
                for row, top, _ in zip(values, tops, indices):
                    last = v.match_replace(row, top[:, first], row, LEAST)
                last.then_inc(vector_step, 1)
                dve.wait_ge(vector_step, steps(t))
                dve.sem_inc(wait_carrier)
                for row, top, _ in zip(values, tops, indices):
                    last = v.max(top[:, second], row)
                last.then_inc(vector_step, 1)
                dve.wait_ge(vector_step, steps(t))
                dve.sem_inc(wait_carrier)
                for row, top, index in zip(values, tops, indices):
                    last = v.max_index(index[:, second], top[:, second], row)
                last.then_inc(vector_step, 1)
                dve.wait_ge(vector_step, steps(t))

            def query(t, i):
                dve.wait_ge(scores_ready, NQ * t + i + 1)
                dve.sem_inc(wait_carrier)
                pair = (2 * i, 2 * i + 1)
                top16(t, [scores[:, s, :] for s in pair], [vtop[:, s, :] for s in pair], [itop[:, s, :] for s in pair])
                dve.sem_inc(wait_carrier)
                v.tensor_tensor(cand[:, i, :].rearrange("p (a b) -> p a b", b=TOPK),
                                vtop[:, 2 * i, :].unsqueeze(2).broadcast_to([P, TOPK, TOPK]),
                                vtop[:, 2 * i + 1, :].unsqueeze(1).broadcast_to([P, TOPK, TOPK]),
                                ALU.add).then_inc(vector_step, 1)
                dve.wait_ge(vector_step, steps(t))
                dve.sem_inc(wait_carrier)
                top16(t, [cand[:, i, :]], [ctop[:, i, :]], [cidx[:, i, :]])

            def pick(t, h0):
                nh = PH // 2
                hs, cols = slice(h0, h0 + nh), slice(h0 * TOPK, (h0 + nh) * TOPK)
                key_numbers = itop_f[:, 2 * h0:2 * (h0 + nh), :]
                v.tensor_copy(key_numbers, itop[:, 2 * h0:2 * (h0 + nh), :]).then_inc(vector_step, 1)
                dve.wait_ge(vector_step, steps(t))
                for half in range(2):
                    if half == 0:
                        ins = v.tensor_scalar(chalf[:, hs, :], cidx[:, hs, :], 4, None, ALU.logical_shift_right)
                    else:
                        ins = v.tensor_scalar(chalf[:, hs, :], cidx[:, hs, :], TOPK - 1, None, ALU.bitwise_and)
                    ins.then_inc(vector_step, 1)
                    dve.wait_ge(vector_step, steps(t))
                    v.tensor_copy(chalf_f[:, half, cols], chalf[:, hs, :].rearrange("p h k -> p (h k)")).then_inc(vector_step, 1)
                    dve.wait_ge(vector_step, steps(t))
                    v.tensor_tensor(onehot[:, hs].rearrange("p h k a -> p (h k) a"),
                                    cst[:, C_IOTA:C_IOTA + TOPK].unsqueeze(1).broadcast_to([P, nh * TOPK, TOPK]),
                                    chalf_f[:, half, cols].unsqueeze(2).broadcast_to([P, nh * TOPK, TOPK]),
                                    ALU.is_equal).then_inc(vector_step, 1)
                    dve.wait_ge(vector_step, steps(t))
                    by_half = key_numbers.rearrange("p (h f) k -> p f h k", f=2)[:, half]
                    v.tensor_tensor(onehot[:, hs], onehot[:, hs], by_half.unsqueeze(2).broadcast_to([P, nh, TOPK, TOPK]),
                                    ALU.mult).then_inc(vector_step, 1)
                    dve.wait_ge(vector_step, steps(t))
                    v.reduce_sum(e_half[:, half, cols], onehot[:, hs].rearrange("p h k a -> p (h k) a"),
                                 AX.X).then_inc(vector_step, 1)
                    dve.wait_ge(vector_step, steps(t))

            def piece_route(t):
                v.tensor_tensor(gate_new[:].rearrange("p (h k) -> p h k", k=TOPK), ctop,
                                ctop[:, :, 0:1].broadcast_to([P, PH, TOPK]), ALU.subtract).then_inc(gate_arg, 1)
                pick(t, PH // 2)
                dve.wait_ge(ids_taken, t)
                v.scalar_tensor_tensor(eid_new[:], e_half[:, 0, :], float(NKEYS), e_half[:, 1, :], ALU.mult,
                                       ALU.add).then_inc(vector_step, 1)
                dve.wait_ge(vector_step, steps(t))
                dve.wait_ge(gate_exp, t + 1)
                by_head = gate_new[:].rearrange("p (h k) -> p h k", k=TOPK)
                v.reduce_sum(g_sum, by_head, AX.X).then_inc(vector_step, 1)
                dve.wait_ge(vector_step, steps(t))
                v.reciprocal(g_inv, g_sum).then_inc(vector_step, 1)
                dve.wait_ge(vector_step, steps(t))
                v.tensor_tensor(by_head, by_head, per_head(g_inv, PH, TOPK), ALU.mult).then_inc(vector_front, 1)
                assert counted[0] == V_STEPS, counted
                counted[0] = 0

            pieces = [piece0, piece1, lambda t: (piece2(t), piece3(t)),
                      lambda t: (level(t, 1), level(t, 2)), lambda t: (level(t, 3), level(t, 4)), lambda t: level(t, 5),
                      lambda t: (piece7(t, 0), piece7(t, 1)), piece8, piece9, lambda t: (piece10(t), residual(t, 0)),
                      lambda t: (residual(t, 1), piece12(t)),
                      lambda t: (query(t, 0), query(t, 1)), lambda t: (query(t, 2), query(t, 3)),
                      lambda t: (query(t, 4), query(t, 5), pick(t, 0)),
                      lambda t: (query(t, 6), query(t, 7), piece_route(t)), lambda t: None]

            def publish(t):
                dve.wait_ge(vector_front, t + 1)
                dve.wait_ge(weights_ready, t * NG)
                v.tensor_copy(xb[:], xb_new[:])
                v.tensor_copy(gate[:], gate_new[:]).then_inc(inputs_ready, 1)
                dve.wait_ge(inputs_ready, t + 1)

            def experts(t, g):
                for j in range(G):
                    dve.wait_ge(u_landed[j], (t * NG + g + 1) * 16)
                    v.tensor_tensor_reduce(u_ring[:, j, :], u_ring[:, j, :], xb[:], 1.0, 0.0, ALU.mult, ALU.add,
                                                hid[:, g * G + j:g * G + j + 1]).then_inc(u_used, 1)
                dve.wait_ge(gelu, t * NG + g + 1)
                v.tensor_tensor(act_w[:, g * G:g * G + G], gel[:, g * G:g * G + G], gate[:, g * G:g * G + G], ALU.mult).then_inc(weights_ready, 1)

            def experts_out(t):
                dve.wait_ge(residual_loaded, (t + 1) * 16)
                dve.wait_ge(v_used, (t + 1) * SLOTS)
                for n in range(2):
                    v.tensor_tensor(h_res[:, n * 512:n * 512 + 512], h_res[:, n * 512:n * 512 + 512],
                                         acc[:, n * 512:n * 512 + 512], ALU.add).then_inc(h2_ready, 1)

            def tile(t):
                for g in range(NG):
                    experts(t - 1, g)
                    if g == 0 and (not isinstance(t, int) or t >= 2):
                        experts_out(t - 2)
                    pieces[g](t)
                publish(t)

            for i in range(NG):
                pieces[i](0)
            publish(0)
            tile(1)
            with dve.Fori(2, NT) as t:
                tile(t)
            for g in range(NG):
                experts(NT - 1, g)
                if g == 0:
                    experts_out(NT - 2)
            experts_out(NT - 1)

            dve.wait_ge(c_w_loaded, 48)
            with dve.Fori(0, NT // 2) as pair:
                t = pair * 2
                for u in range(2):
                    k = t + u
                    dve.wait_ge(row_squares, 2 * NT + k + 1)
                    mean_to_ms(c_rs, c_ss, D).then_inc(mean_square, 1)
                    dve.wait_ge(root, 5 * NT + k + 1)
                    v.reciprocal(c_rs, c_rs).then_inc(inverse_root, 1)
                    dve.wait_ge(inverse_root, NT + k + 1)
                    v.scalar_tensor_tensor(c_n[:], c_h[u][:], c_rs, g_ple_b[:], ALU.mult, ALU.mult).then_inc(xb_ready, 1)
                    dve.wait_ge(c_pT_turned, k + 1)
                    v.tensor_copy(c_pT[:].rearrange("p c n -> p (c n)"), bank[2][:, 0:PLE]).then_inc(c_pT_ready, 1)
                    dve.wait_ge(rows_stored[u], 8 * NT + t * 8)
                    dve.wait_ge(c_proj_mm, k + 1)
                    dve.wait_ge(c_gate, 2 * k + 2)
                    v.tensor_tensor(c_o[u][:], c_e[:], acc[:, :], ALU.mult).then_inc(c_gated, 1)
                    dve.wait_ge(c_gated, k + 1)
                    v.tensor_tensor(c_o[u][:], c_o[u][:], c_h[u][:], ALU.add).then_inc(c_out_ready, 1)


_INS = ["x", "p", "g_mix", "w_in", "gdn_conv_w", "gdn_a_log", "gdn_dt_bias", "gdn_norm_g", "swa_q_norm_g", "swa_k_norm_g",
        "swa_sinks", "rel_bias", "w_out", "g_ffn", "peer_w_query", "peer_sub_keys", "peer_u", "peer_v", "g_ple",
        "ple_w_gate", "ple_w_proj"]


def kernel(**inputs):
    import concourse.bacc as _bacc
    from concourse.bass_utils import run_bass_kernel_spmd as _run

    nc = _bacc.Bacc("TRN2", target_bir_lowering=False, num_devices=1)
    arrays, args = {}, []
    for name in _INS + ["consts"]:
        a = constants() if name == "consts" else np.ascontiguousarray(inputs[name])
        arrays[f"in_{name}_dram"] = a
        args.append(nc.dram_tensor(f"in_{name}_dram", a.shape, mybir.dt.from_np(a.dtype), kind="ExternalInput").ap())
    out = nc.dram_tensor("out_0_dram", (1, SEQ, D), F32, kind="ExternalOutput").ap()
    block_kernel(nc, *args, out)
    r = _run(nc, [arrays], core_ids=[0])
    return r.results[0]["out_0_dram"]
```

```python
from contextlib import ExitStack

import numpy as np

import concourse.bass as bass
from concourse import mybir

ALU = mybir.AluOpType
ACT = mybir.ActivationFunctionType
AX = mybir.AxisListType
F32 = mybir.dt.float32
U32 = mybir.dt.uint32

P = 128
D = 1024
DC = D // P
SEQ = 1024
NT = SEQ // P
CHUNK = 64
HD = 64
NH = 8
NKV = 2
GW = NH * HD
QKV = 3 * GW
TOKW = 2832 - QKV
Z0, B0, A0, SQ0, SK0, SV0 = 0, 512, 520, 528, 1040, 1168
CONV = 4
WIN = CHUNK + P
LEVELS = 6
EPS = 1e-6
MASKED = -1e30
REL_BUCKETS, REL_MAX_DIST = 32, 128
RELS = 320
PLE = 256
PH = 8
NKEYS = 128
TOPK = 16
NHH = 2 * PH
SLOTS = PH * TOPK
G = 8
NG = SLOTS // G
QCOL = 256
NQ = PH * 2 * 128 // QCOL
LEAST = -3.0e38
V_STEPS = 99
V_FIRST = 16
FIRST = 2
EARLY = 2 * TOPK // G

C_ID, C_TRIL, C_BLOCK, C_ONES, C_CH0, C_CH1 = (P * i for i in range(6))
C_LEVEL = 6 * P
C_WIN = C_LEVEL + LEVELS * P
C_IOTA = C_WIN + WIN
C_REL = C_IOTA + TOPK
C_ALL = C_REL + RELS


def t5_bucket(rel):
    half = REL_BUCKETS // 2
    exact = half // 2
    n = np.abs(rel)
    large = exact + (np.log(np.maximum(n, 1) / exact) / np.log(REL_MAX_DIST / exact) * (half - exact)).astype(np.int32)
    return (rel > 0).astype(np.int32) * half + np.where(n < exact, n, np.minimum(large, half - 1)).astype(np.int32)


def constants():
    c = np.zeros((P, C_ALL), np.float32)
    i = np.arange(P)
    row, col = i[:, None], i[None, :]
    same = row // CHUNK == col // CHUNK
    c[:, C_ID:C_ID + P] = row == col
    c[:, C_TRIL:C_TRIL + P] = same & (row <= col)
    c[:, C_BLOCK:C_BLOCK + P] = same
    c[:, C_ONES:C_ONES + P] = 1.0
    c[:CHUNK, C_CH0:C_CH0 + P] = 1.0
    c[CHUNK:, C_CH1:C_CH1 + P] = 1.0
    for l in range(LEVELS):
        at = C_LEVEL + l * P
        c[:, at:at + P] = (row >> (l + 1) == col >> (l + 1)) & ((col >> l) & 1 == 1) & ((row >> l) & 1 == 0)
    w = np.arange(WIN)[None, :]
    seen = np.where(row < CHUNK, w < 2 * CHUNK, w >= CHUNK)
    c[:, C_WIN:C_WIN + WIN] = np.where(seen, 0.0, MASKED)
    c[:, C_IOTA:C_IOTA + TOPK] = np.arange(TOPK)
    rel = np.arange(RELS) - (WIN - 1)
    c[:REL_BUCKETS, C_REL:C_REL + RELS] = t5_bucket(rel)[None, :] == np.arange(REL_BUCKETS)[:, None]
    return c


def block_kernel(nc, x, p, g_mix, w_in, gdn_conv_w, gdn_a_log, gdn_dt_bias, gdn_norm_g, swa_q_norm_g, swa_k_norm_g,
                 swa_sinks, rel_bias, w_out, g_ffn, peer_w_query, peer_sub_keys, peer_u, peer_v, g_ple, ple_w_gate,
                 ple_w_proj, consts, out):
    x, p, out = x[0], p[0, 0], out[0]
    w_in, w_out, w_query = w_in[0], w_out[0], peer_w_query[0]
    sub_keys, table_u, table_v = peer_sub_keys[0], peer_u[0], peer_v[0]
    w_gate, w_proj, conv_w = ple_w_gate[0], ple_w_proj[0], gdn_conv_w[0]

    conv_dram = nc.dram_tensor("conv_scratch", (QKV, SEQ), F32, kind="Internal").ap()
    tok_dram = nc.dram_tensor("tok_scratch", (SEQ, TOKW), F32, kind="Internal").ap()
    h2_dram = nc.dram_tensor("h2_scratch", (SEQ, D), F32, kind="Internal").ap()
    rel_dram = nc.dram_tensor("rel_scratch", (NH, P, RELS), F32, kind="Internal").ap()

    with ExitStack() as ctx:
        def signal(name):
            return ctx.enter_context(nc.semaphore(name))

        consts_loaded = signal("consts_loaded")
        g_mix_loaded = signal("g_mix_loaded")
        taps_loaded = signal("taps_loaded")
        a_w_loaded = [signal(f"a_w_loaded{n}") for n in range(3)]
        params_b = signal("params_b")
        a_tok_ready = signal("a_tok_ready")
        a_n_ready = signal("a_n_ready")
        a_conv_ready = signal("a_conv_ready")
        a_conv_stored = [signal(f"a_conv_stored{u}") for u in range(2)]
        a_channels_mm = signal("a_channels_mm")
        a_nT_ready = signal("a_nT_ready")
        a_nT_copied = signal("a_nT_copied")
        a_tok_mm = signal("a_tok_mm")
        a_halo_zero = signal("a_halo_zero")
        a_in_ready = signal("a_in_ready")
        a_conv_sum = signal("a_conv_sum")
        a_turned = signal("a_turned")
        inverse_root = signal("inverse_root")
        keys_loaded = signal("keys_loaded")
        w_out_loaded = signal("w_out_loaded")
        rel_rows_ready = signal("rel_rows_ready")
        rel_stored = signal("rel_stored")
        bias_loaded = signal("bias_loaded")
        keysT_ready = signal("keysT_ready")
        keys_T = signal("keys_T")
        rel_mm = signal("rel_mm")
        rate_exp = signal("rate_exp")
        rate_ready = signal("rate_ready")
        bias_ready = signal("bias_ready")
        c_w_loaded = signal("c_w_loaded")
        c_gain_loaded = signal("c_gain_loaded")
        c_out_ready = signal("c_out_ready")
        c_gate = signal("c_gate")
        c_pT_turned = signal("c_pT_turned")
        c_pT_ready = signal("c_pT_ready")
        c_proj_mm = signal("c_proj_mm")
        c_gated = signal("c_gated")
        gelu = signal("gelu")
        ids_taken = signal("ids_taken")
        first_ids_ready = signal("first_ids_ready")
        first_ids_taken = signal("first_ids_taken")
        inputs_ready = signal("inputs_ready")
        h2_stored = signal("h2_stored")
        h1_added = signal("h1_added")
        h2_ready = signal("h2_ready")
        group_ids_ready = signal("group_ids_ready")
        u_used = signal("u_used")
        u_landed = [signal(f"u_landed{u}") for u in range(G)]
        v_used = signal("v_used")
        v_landed = [signal(f"v_landed{u}") for u in range(G)]
        weights_ready = signal("weights_ready")
        diag_ready = signal("diag_ready")
        s_exp = signal("s_exp")
        rows_in = [signal(f"rows_in{u}") for u in range(2)]
        rows_stored = [signal(f"rows_stored{u}") for u in range(2)]
        wq_loaded = [signal(f"wq_loaded{u}") for u in range(2)]
        vector_front = signal("vector_front")
        qkv_loaded = signal("qkv_loaded")
        tok_loaded = signal("tok_loaded")
        squares = signal("squares")
        s_T = signal("s_T")
        s_T_out = signal("s_T_out")
        x_loaded = signal("x_loaded")
        h1_ready = signal("h1_ready")
        query_mm = signal("query_mm")
        row_squares = signal("row_squares")
        mean_square = signal("mean_square")
        root = signal("root")
        qkv_tok = signal("qkv_tok")
        beta_exp = signal("beta_exp")
        x_abs = signal("x_abs")
        x_exp = signal("x_exp")
        softplus_tail = signal("softplus_tail")
        gcs_ready = signal("gcs_ready")
        k_gap = signal("k_gap")
        decays = signal("decays")
        dec_arg = signal("dec_arg")
        dec_exp = signal("dec_exp")
        heads_T = signal("heads_T")
        heads_T_out = signal("heads_T_out")
        inv_turned = signal("inv_turned")
        inv_ready = signal("inv_ready")
        qkT_ready = signal("qkT_ready")
        level_x = signal("level_x")
        level_x_out = signal("level_x_out")
        nw_mm = signal("nw_mm")
        nw_out = signal("nw_out")
        u_mm = signal("u_mm")
        u_out = signal("u_out")
        silu_z = signal("silu_z")
        o_inter_mm = signal("o_inter_mm")
        o_inter_out = signal("o_inter_out")
        o_sum = signal("o_sum")
        o_squares = signal("o_squares")
        o_T = signal("o_T")
        mix_ready = signal("mix_ready")
        s_squares = signal("s_squares")
        window_moved = signal("window_moved")
        s_max = signal("s_max")
        probs_T = signal("probs_T")
        probsT_ready = signal("probsT_ready")
        av_mm = signal("av_mm")
        n2_T = signal("n2_T")
        n2T_ready = signal("n2T_ready")
        qr_ready = signal("qr_ready")
        qr_T = signal("qr_T")
        qrT_ready = signal("qrT_ready")
        score_mm = signal("score_mm")
        scores_ready = signal("scores_ready")
        gate_arg = signal("gate_arg")
        gate_exp = signal("gate_exp")
        g_ready = signal("g_ready")
        h1_mm = signal("h1_mm")
        cumsum = signal("cumsum")
        gdiag_ready = signal("gdiag_ready")
        gc_rows = signal("gc_rows")
        scaled = signal("scaled")
        invT_ready = signal("invT_ready")
        kk_mm = signal("kk_mm")
        qk_mm = signal("qk_mm")
        level_p = signal("level_p")
        state_ready = signal("state_ready")
        ws_mm = signal("ws_mm")
        v_new_ready = signal("v_new_ready")
        kv_mm = signal("kv_mm")
        o_intra_mm = signal("o_intra_mm")
        o_normed = signal("o_normed")
        s_normed = signal("s_normed")
        logits_mm = signal("logits_mm")
        probs_ready = signal("probs_ready")
        xb_ready = signal("xb_ready")
        vector_step = signal("vector_step")
        wait_carrier = signal("wait_carrier")

        def sb(where, name, shape, dt=F32):
            return where.enter_context(nc.sbuf_tensor(name, shape, dt))


        bank = [ctx.enter_context(nc.psum_tensor(f"bank{i}", [P, 512], F32)) for i in range(6)]
        acc = ctx.enter_context(nc.psum_tensor("expert_sum", [P, D], F32))

        cst = sb(ctx, "constants", [P, C_ALL])
        ident = cst[:, C_ID:C_ID + P]
        g_mix_c = sb(ctx, "g_mix_by_channel", [P, DC])
        conv_c = sb(ctx, "conv_by_channel", [P, CONV, QKV // P])
        q_gain = sb(ctx, "swa_q_gain", [P, 1])
        k_gain = sb(ctx, "swa_k_gain", [P, 1])
        norm_g = sb(ctx, "gdn_norm_gain", [P, HD])
        a_rate = sb(ctx, "a_log_rows", [P, NH])
        neg_rate = sb(ctx, "minus_exp_a_log", [P, NH])
        dt_row = sb(ctx, "dt_bias_rows", [P, NH])
        sinks = sb(ctx, "sink_rows", [P, NH])
        small = sb(ctx, "small", [P, 280])
        rel_sb = sb(ctx, "rel_bias_sb", [REL_BUCKETS, NH])
        bias_t = sb(ctx, "swa_bias", [P, NH, WIN])

        with ExitStack() as a_ctx:
            a_w = sb(a_ctx, "w_token", [P, DC, TOKW])
            a_nT = sb(a_ctx, "normed_by_channel", [P, DC, SEQ])
            a_x = [sb(a_ctx, f"x_in{u}", [P, D]) for u in range(2)]
            a_n = [sb(a_ctx, f"x_normed{u}", [P, D]) for u in range(2)]
            a_nTt = [sb(a_ctx, f"normed_tile{u}", [P, DC, P]) for u in range(2)]
            a_tok = [sb(a_ctx, f"token_out{u}", [P, TOKW]) for u in range(2)]
            a_wc = [sb(a_ctx, f"w_channel{u}", [P, DC, P]) for u in range(2)]
            a_in = [sb(a_ctx, f"conv_in{u}", [P, CONV - 1 + SEQ]) for u in range(2)]
            a_cv = [sb(a_ctx, f"conv_sum{u}", [P, SEQ]) for u in range(2)]
            a_out = [sb(a_ctx, f"conv_out{u}", [P, SEQ]) for u in range(2)]
        with ExitStack() as b_ctx:
            KB = 256
            arena = sb(b_ctx, "arena", [P, 49 * KB + 64])
            wq = [sb(b_ctx, f"w_query{u}", [P, DC, QCOL]) for u in range(2)]
            u_ring = sb(b_ctx, "u_rows", [P, G, D])
            v_ring = sb(b_ctx, "v_rows", [P, G, D])
            xb_new = sb(b_ctx, "ffn_in_new", [P, D])
            xb = sb(b_ctx, "ffn_in", [P, D])
            diag = sb(b_ctx, "weight_diagonals", [P, G, P])
            h2_sb = xb_new
            w_out_sb = sb(b_ctx, "w_out_sb", [P, DC, D])
            keysT = sb(b_ctx, "keys_by_channel", [P, NHH, P])
            g_ffn_b = sb(b_ctx, "g_ffn_rows", [P, D])
            eid_new = sb(b_ctx, "expert_id_new", [P, SLOTS])
            eid = sb(b_ctx, "expert_id", [P, SLOTS], U32)
            gate_new = sb(b_ctx, "gate_new", [P, SLOTS])
            gate = sb(b_ctx, "gate", [P, SLOTS])
            hid = sb(b_ctx, "hidden", [P, SLOTS])
            gel = sb(b_ctx, "gelu", [P, SLOTS])
            act_w = sb(b_ctx, "expert_weight", [P, SLOTS])
            ids = sb(b_ctx, "group_ids", [P, 2, G], U32)
            state = sb(b_ctx, "gdn_state", [P, 4, HD])
            kwin = sb(b_ctx, "key_window", [P, WIN])
            vprev = sb(b_ctx, "values_before", [P, P])
            vcur = sb(b_ctx, "values_here", [P, P])

        def part(kb, cols):
            return arena[:, int(kb * KB):int(kb * KB) + cols]

        keys_in = part(0, NHH * P).rearrange("p (s n) -> p s n", n=P)
        rel_rows = part(8, NH * RELS).rearrange("p (h r) -> p h r", h=NH)
        qkv_in = part(0, QKV).rearrange("p (c n) -> p c n", n=P)
        tokp = part(6, TOKW)
        x_t = part(2, D)
        kn, nkb, qn, qg = (part(11.25 + 2 * i, GW) for i in range(4))
        vb, nkbg, kdec = (part(19.25 + 2 * i, GW) for i in range(3))
        knT, nkbT, qnT, qgT = (part(25.25 + 2 * i, GW).rearrange("p (q n) -> p q n", n=P) for i in range(4))
        decT = part(33.25, 8 * P).rearrange("p (s n) -> p s n", n=P)
        amT = part(37.25, 8 * P).rearrange("p (s n) -> p s n", n=P)
        square = part(37.25, 8 * P)
        qkT = part(41.25, 8 * P).rearrange("p (s n) -> p s n", n=P)
        gdiag = part(41.25, 8 * P).rearrange("p (s n) -> p s n", n=P)
        mixT = part(45.25, 8 * P).rearrange("p (s n) -> p s n", n=P)
        invT = part(11.25, 8 * P).rearrange("p (s n) -> p s n", n=P)
        step_x = part(15.25, 8 * P).rearrange("p (s n) -> p s n", n=P)
        inv = decT
        nwT, u_sb, v_new, o_inter = knT, part(27.25, GW), part(29.25, GW), part(0, GW)
        o_sb, zs, o_sq = part(2, GW), part(4, GW), part(15.25, GW)
        s_n = part(33.25, 10 * HD)
        s_sq = part(37.25, 10 * HD)
        sqT = part(19.25, GW).rearrange("p (q n) -> p q n", n=P)
        probs = part(11.25, NH * 256).rearrange("p (h n) -> p h n", n=256)
        probsT = part(25.25, 16 * P).rearrange("p (s n) -> p s n", n=P)
        h1 = part(11.25, D)
        n2T = part(15.25, D).rearrange("p (c n) -> p c n", n=P)
        h_junk = part(0, D)
        qr = [part(19.25 + u, QCOL) for u in range(2)]
        qrT = [part(21.25 + u, QCOL).rearrange("p (s n) -> p s n", n=P) for u in range(2)]
        scores = part(25.25, NHH * P).rearrange("p (s n) -> p s n", n=P)
        cand = part(33.25, PH * 256).rearrange("p (h n) -> p h n", n=256)
        onehot = part(41.25, 2 * D).rearrange("p (h k a) -> p h k a", h=PH, k=TOPK)
        vtop = part(4, NHH * TOPK).rearrange("p (s k) -> p s k", k=TOPK)
        itop = part(5, NHH * TOPK).rearrange("p (s k) -> p s k", k=TOPK).bitcast(U32)
        itop_f = part(6, NHH * TOPK).rearrange("p (s k) -> p s k", k=TOPK)
        ctop = part(7, SLOTS).rearrange("p (h k) -> p h k", k=TOPK)
        cidx = part(7.5, SLOTS).rearrange("p (h k) -> p h k", k=TOPK).bitcast(U32)
        chalf = part(8, SLOTS).rearrange("p (h k) -> p h k", k=TOPK).bitcast(U32)
        chalf_f = part(8.5, 2 * SLOTS).rearrange("p (f s) -> p f s", f=2)
        e_half = part(9.5, 2 * SLOTS).rearrange("p (f s) -> p f s", f=2)
        wg_sb = w_out_sb
        wp_sb = wq[0][:].rearrange("p c n -> p (c n)").rearrange("p (c n) -> p c n", n=D)
        c_h = [part(4 * u, D) for u in range(2)]
        c_p = [part(8 + u, PLE) for u in range(2)]
        c_pT = part(10, PLE).rearrange("p (c n) -> p c n", n=P)
        c_nT = part(16, D).rearrange("p (c n) -> p c n", n=P)
        c_e, c_n, c_junk, g_ple_b = part(20, D), part(24, D), part(36, D), part(40, D)
        c_o = [part(28 + 4 * u, D) for u in range(2)]
        ssq, rst = small[:, 0:16], small[:, 16:32]
        beta, nbeta, gl, eg, kd = (small[:, 32 + 8 * i:40 + 8 * i] for i in range(5))
        xa, xabs, e2 = (small[:, 72 + 8 * i:80 + 8 * i] for i in range(3))
        gcs = small[:, 96:128]
        glp = small[:, 128:136].rearrange("p (c q) -> p c q", c=2)
        kgap = small[:, 136:144]
        s_ss, s_rs = small[:, 144:154], small[:, 154:164]
        s_m, s_nm, s_den, s_es, s_gap = (small[:, 164 + 8 * i:172 + 8 * i] for i in range(5))
        h_ss, h_rs = small[:, 204:205], small[:, 205:206]
        g_sum, g_inv = small[:, 206:214], small[:, 214:222]
        o_ss, o_rs = small[:, 222:230], small[:, 230:238]
        a_ss, a_rs = small[:, 240:242], small[:, 248:250]
        c_ss, c_rs = small[:, 256:257], small[:, 257:258]
        spl = small[:, 260:268]
        eb = small[:, 268:276]

        def heads(ap, n=NH):
            return ap.rearrange("p (h d) -> p h d", h=n)

        def per_head(ap, n=NH, width=HD):
            return ap.unsqueeze(2).broadcast_to([P, n, width])

        def norm_of(t, i):
            return NT + 4 * t + i

        def ple_rows(k):
            return h2_sb[:] if k == NT - 1 else c_h[k % 2]

        def ple_loaded(k):
            return 8 * NT + 32 * (k // 2 + 1) - (16 if k == NT - 1 else 0)

        def merged(pieces):
            return [pieces[0:2]] + [[piece] for piece in pieces[2:6]] + [pieces[6:8]] + [[piece] for piece in pieces[8:]]

        block = ctx.enter_context(nc.Block())
        bias_banks = (3, 4, 5, 0)

        @block.sync
        def _(sp):
            for u in range(2):
                sp.dma_start(a_x[u][:], x[u * P:u * P + P, :]).then_inc(rows_in[u], 16)
            sp.dma_start(cst[:], consts).then_inc(consts_loaded, 16)
            with nc.allow_non_contiguous_dma("vectors of parameters, a few KB, loaded once"):
                sp.dma_start(g_mix_c[:], g_mix[0].rearrange("(c p) -> p c", p=P)).then_inc(g_mix_loaded, 16)
                w_in_v = w_in.rearrange("(c p) n -> p c n", p=P)
                for n in range(3):
                    cols = slice(n * 512, min(n * 512 + 512, TOKW))
                    sp.dma_start(a_w[:, :, cols], w_in_v[:, :, QKV:QKV + TOKW][:, :, cols]).then_inc(a_w_loaded[n], 16)
                for k in range(CONV):
                    sp.dma_start(conv_c[:, k, :], conv_w[k].rearrange("(c p) -> p c", p=P)).then_inc(taps_loaded, 16)
                for kv in range(NKV):
                    sp.dma_start(q_gain[kv * HD:kv * HD + HD, :], swa_q_norm_g.rearrange("a d -> d a")).then_inc(params_b, 16)
                    sp.dma_start(k_gain[kv * HD:kv * HD + HD, :], swa_k_norm_g.rearrange("a d -> d a")).then_inc(params_b, 16)
            sp.dma_start(norm_g[:], gdn_norm_g.broadcast_to([P, HD])).then_inc(params_b, 16)
            sp.dma_start(a_rate[:], gdn_a_log.broadcast_to([P, NH])).then_inc(params_b, 16)
            sp.dma_start(dt_row[:], gdn_dt_bias.broadcast_to([P, NH])).then_inc(params_b, 16)
            sp.dma_start(sinks[:], swa_sinks.broadcast_to([P, NH])).then_inc(params_b, 16)
            sp.dma_start(rel_sb[:], rel_bias).then_inc(params_b, 16)

            def store_tokens(t, u):
                sp.wait_ge(a_tok_ready, (t + u + 1) * 3)
                sp.dma_start(tok_dram[bass.ds((t + u) * P, P), :], a_tok[u][:]).then_inc(rows_stored[u], 16)

            with sp.Fori(0, NT // 2 - 1) as pair:
                t = pair * 2
                for u in range(2):
                    sp.wait_ge(a_n_ready, t + u + 1)
                    sp.dma_start(a_x[u][:], x[bass.ds((t + u + 2) * P, P), :]).then_inc(rows_in[u], 16)
                    store_tokens(t, u)
            for u in range(2):
                sp.dma_start(a_wc[u][:], w_in_v[:, :, u * P:u * P + P]).then_inc(wq_loaded[u], 16)
            for u in range(2):
                store_tokens(NT - 2, u)

            def store_channels(ct, u):
                sp.wait_ge(a_conv_ready, ct + u + 1)
                sp.dma_start(conv_dram[bass.ds((ct + u) * P, P), :], a_out[u][:]).then_inc(a_conv_stored[u], 16)

            def channel_pair(ct):
                for u in range(2):
                    sp.wait_ge(a_channels_mm, (ct + u + 1) * 2)
                    sp.dma_start(a_wc[u][:], w_in_v[:, :, bass.ds((ct + u + 2) * P, P)]).then_inc(wq_loaded[u], 16)
                    store_channels(ct, u)

            sp.wait_ge(a_tok_mm, 3 * NT)
            sp.dma_start(keys_in, sub_keys.rearrange("f h n d -> n (f h) d")).then_inc(keys_loaded, 16)
            sp.dma_start(w_out_sb[:], w_out.rearrange("(c p) n -> p c n", p=P)).then_inc(w_out_loaded, 16)
            sp.dma_start(g_ffn_b[:], g_ffn.broadcast_to([P, D])).then_inc(w_out_loaded, 16)
            channel_pair(0)
            sp.wait_ge(rel_rows_ready, NH)
            sp.dma_start(rel_dram.rearrange("h p r -> p h r"), rel_rows).then_inc(rel_stored, 16)
            with sp.Fori(1, QKV // P // 2 - 1) as pair:
                channel_pair(pair * 2)
            for u in range(2):
                store_channels(QKV // P - 2, u)
            sp.wait_ge(rel_stored, 16)
            sp.dma_start(bias_t[:], bass.AP(tensor=rel_dram.tensor, offset=WIN - 1 - CHUNK,
                                            ap=[[RELS - 1, P], [P * RELS, NH], [1, WIN]])).then_inc(bias_loaded, 16)
            for u in range(2):
                sp.wait_ge(rows_stored[u], 16 * NT // 2)
                sp.wait_ge(a_conv_stored[u], 16 * QKV // P // 2)
            sp.wait_ge(keysT_ready, 4)

            def experts_store(t):
                sp.wait_ge(h2_ready, (t + 1) * 2)
                sp.dma_start(h2_dram[bass.ds(t * P, P), :], h2_sb[:]).then_inc(h2_stored, 16)

            def front_loads(t):
                at = bass.ds(t * P, P)
                sp.wait_ge(vector_front, t)
                sp.sem_inc(wait_carrier)
                sp.dma_start(qkv_in, conv_dram.rearrange("(c p) n -> p c n", p=P)[:, :, at]).then_inc(qkv_loaded, 16)
                sp.dma_start(tokp, tok_dram[at, :]).then_inc(tok_loaded, 16)
                for i in range(NQ):
                    if i == 1:
                        if not isinstance(t, int) or t >= 2:
                            experts_store(t - 2)
                        sp.wait_ge(mix_ready, 2 * t + 1)
                        sp.dma_start(x_t, x[at, :]).then_inc(x_loaded, 16)
                    if i >= 2:
                        sp.wait_ge(query_mm, t * NQ + i - 1)
                    sp.dma_start(wq[i % 2][:], w_query.rearrange("(c p) n -> p c n", p=P)[:, :, i * QCOL:(i + 1) * QCOL]
                                 ).then_inc(wq_loaded[i % 2], 16)

            front_loads(0)
            front_loads(1)
            with sp.Fori(2, NT) as t:
                front_loads(t)

            def ple_loads(k):
                if k < NT - 1:
                    sp.dma_start(c_h[k % 2], h2_dram[k * P:k * P + P, :]).then_inc(rows_in[k % 2], 16)
                sp.dma_start(c_p[k % 2], p[k * P:k * P + P, :]).then_inc(rows_in[k % 2], 16)

            sp.wait_ge(vector_front, NT)
            sp.wait_ge(h2_stored, 16 * (NT - 2))
            sp.dma_start(g_ple_b, g_ple.broadcast_to([P, D])).then_inc(c_gain_loaded, 16)
            for k in range(2):
                ple_loads(k)
            sp.dma_start(wp_sb, w_proj.rearrange("(c p) n -> p c n", p=P)).then_inc(c_w_loaded, 16)
            sp.dma_start(wg_sb[:], w_gate.rearrange("(c p) n -> p c n", p=P)).then_inc(c_w_loaded, 16)
            experts_store(NT - 2)
            sp.wait_ge(h2_stored, 16 * (NT - 1))
            for k in range(NT):
                sp.wait_ge(c_out_ready, k + 1)
                sp.dma_start(out[k * P:k * P + P, :], c_o[k % 2]).then_inc(rows_stored[k % 2], 16)
                if k + 2 < NT:
                    ple_loads(k + 2)
            for u in range(2):
                sp.wait_ge(rows_stored[u], 16 * NT)

        @block.gpsimd
        def _(pool):
            def gather_group(t, g, half):
                n = t * SLOTS + g * G
                first = isinstance(g, int) and g == 0 and isinstance(t, int)
                nc.gpsimd.tensor_copy(ids[:, half, :], eid[:, bass.ds(g * G, G)]).then_inc(group_ids_ready, 1)
                pool.wait_ge(group_ids_ready, t * NG + g + 1)
                pool.sem_inc(wait_carrier)
                for table, ring, used, landed in ((table_u, u_ring, u_used, u_landed), (table_v, v_ring, v_used, v_landed)):
                    for j in range(G):
                        if j % 2 == 0 and not first:
                            pool.wait_ge(used, n - G + j + 2)
                            pool.sem_inc(wait_carrier)
                        nc.gpsimd.indirect_dma_start(
                            ring[:, j, :], None, table, bass.IndirectOffsetOnAxis(ids[:, half, j:j + 1], 0)).then_inc(landed[j], 16)

            def take_ids(t):
                pool.wait_ge(vector_front, t + 1)
                pool.sem_inc(wait_carrier)
                nc.gpsimd.tensor_copy(eid[:], eid_new[:]).then_inc(ids_taken, 1)
                pool.wait_ge(ids_taken, t + 1)

            pool.wait_ge(first_ids_ready, 1)
            nc.gpsimd.tensor_copy(eid[:, 0:EARLY * G], eid_new[:, 0:EARLY * G]).then_inc(first_ids_taken, 1)
            pool.wait_ge(first_ids_taken, 1)
            for g in range(EARLY):
                gather_group(0, g, g % 2)
            take_ids(0)
            with pool.Fori(EARLY // 2, NG // 2) as pair:
                g = pair * 2
                for half in range(2):
                    gather_group(0, g + half, half)
            with pool.Fori(1, NT) as t:
                take_ids(t)
                pool.sem_inc(wait_carrier)
                with pool.Fori(0, NG // 2) as pair:
                    g = pair * 2
                    for half in range(2):
                        gather_group(t, g + half, half)

        @block.scalar
        def _(act):
            def f(out_, in_, func, **kw):
                return nc.scalar.activation(out_, in_, func, **kw)

            def token_norm(t, u):
                act.wait_ge(rows_in[u], t * 8 + 16)
                f(a_cv[u][:], a_x[u][:], ACT.Square, accum_out=a_ss[:, u:u + 1]).then_inc(row_squares, 1)
                act.wait_ge(mean_square, t + u + 1)
                f(a_rs[:, u:u + 1], a_rs[:, u:u + 1], ACT.Sqrt).then_inc(root, 1)

            def token_out(t, u, more=True):
                act.wait_ge(a_nT_ready, (t + u + 1) * 2)
                nc.scalar.copy(a_nT[:, :, bass.ds((t + u) * P, P)], a_nTt[u][:]).then_inc(a_nT_copied, 1)
                for n, width in enumerate((512, 512, TOKW - 1024)):
                    act.wait_ge(a_tok_mm, (t + u) * 3 + n + 1)
                    if n == 0:
                        act.wait_ge(rows_stored[u], t * 8)
                    nc.scalar.copy(a_tok[u][:, n * 512:n * 512 + width], bank[2 + n][:, 0:width]).then_inc(a_tok_ready, 1)
                    if n == 0 and more:
                        token_norm(t + 2, u)

            for u in range(2):
                token_norm(0, u)
            for u in range(2):
                token_out(0, u)
            with act.Fori(1, NT // 2 - 1) as pair:
                for u in range(2):
                    token_out(pair * 2, u)
            for u in range(2):
                token_out(NT - 2, u, False)

            act.wait_ge(a_halo_zero, 1)
            def channel_pair(ct):
                for u in range(2):
                    for half in range(2):
                        act.wait_ge(a_channels_mm, (ct + u) * 2 + half + 1)
                        nc.scalar.copy(a_in[u][:, CONV - 1 + half * 512:CONV - 1 + half * 512 + 512],
                                            bank[2 * u + half][:, :]).then_inc(a_in_ready, 1)
                    act.wait_ge(a_conv_sum, (ct + u + 1) * CONV)
                    act.wait_ge(a_conv_stored[u], ct * 8)
                    f(a_out[u][:], a_cv[u][:], ACT.Silu).then_inc(a_conv_ready, 1)

            channel_pair(0)
            for b in range(4):
                act.wait_ge(keys_T, b + 1)
                half, h0 = b // 2, (b % 2) * 4
                nc.scalar.copy(keysT[:].rearrange("p (h f) n -> p f h n", f=2)[:, half, h0:h0 + 4, :],
                               bank[4 + b % 2][:, :].rearrange("p (h n) -> p h n", n=P)).then_inc(keysT_ready, 1)
            for h in range(NH):
                act.wait_ge(rel_mm, h + 1)
                nc.scalar.copy(rel_rows[:, h, :], bank[4 + h % 2][:, 0:RELS]).then_inc(rel_rows_ready, 1)
            with act.Fori(1, QKV // P // 2) as pair:
                channel_pair(pair * 2)

            act.wait_ge(params_b, 16 * 9)
            f(neg_rate[:], a_rate[:], ACT.Exp).then_inc(rate_exp, 1)

            def norm_root(n, ap):
                act.wait_ge(mean_square, n + 1)
                f(ap, ap, ACT.Sqrt).then_inc(root, 1)

            def piece0(t):
                act.wait_ge(vector_front, t)
                for i in range(2):
                    act.wait_ge(qkv_tok, 3 * t + i + 1)
                    f(square[:, i * GW:i * GW + GW], bank[i][:, :], ACT.Square).then_inc(squares, 1)
                norm_root(norm_of(t, 0), rst)

            def piece1(t):
                act.wait_ge(tok_loaded, (t + 1) * 16)
                f(eb, tokp[:, B0:B0 + NH], ACT.Exp, scale=-1.0).then_inc(beta_exp, 1)
                act.wait_ge(x_abs, t + 1)
                f(e2, xabs, ACT.Exp, scale=-1.0).then_inc(x_exp, 1)
                act.wait_ge(x_exp, t + 1)
                f(spl, e2, ACT.Ln, bias=1.0).then_inc(softplus_tail, 1)

            def decays_of(t):
                act.wait_ge(gcs_ready, t + 1)
                f(eg, gcs[:, 0:NH], ACT.Exp)
                pairs = gcs[:, 16:32].rearrange("p (c q r) -> p r c q", c=2, r=2)
                for r in range(2):
                    f(glp[r * HD:r * HD + HD], pairs[r * HD:r * HD + HD, r], ACT.Exp)
                act.wait_ge(k_gap, t + 1)
                f(kd, kgap, ACT.Exp).then_inc(decays, 1)
                act.wait_ge(dec_arg, t + 1)
                f(decT, decT, ACT.Exp).then_inc(dec_exp, 1)

            def piece2(t):
                for i, (dst, b) in enumerate(((knT, 3), (nkbT, 4), (qnT, 5), (qgT, 0))):
                    act.wait_ge(heads_T, 4 * t + i + 1)
                    nc.scalar.copy(dst.rearrange("p q n -> p (q n)"), bank[b][:, :]).then_inc(heads_T_out, 1)

            def inverse_out(t, n):
                for r in range(2):
                    act.wait_ge(inv_turned, 10 * t + n + r + 1)
                    nc.scalar.copy(inv[:, 4 * r:4 * r + 4, :].rearrange("p s n -> p (s n)"),
                                        bank[(0, 5)[r]][:, :]).then_inc(inv_ready, 1)

            def piece3(t):
                act.wait_ge(qkT_ready, 2 * t + 2)
                inverse_out(t, 0)

            def level(t, l):
                for r in range(2):
                    act.wait_ge(level_x, 10 * t + 2 * (l - 1) + r + 1)
                    nc.scalar.copy(step_x[:, 4 * r:4 * r + 4, :].rearrange("p s n -> p (s n)"),
                                        bank[1 + r][:, :]).then_inc(level_x_out, 1)
                if l < LEVELS - 1:
                    inverse_out(t, 2 * l)

            def piece6(t):
                level(t, 5)
                act.wait_ge(nw_mm, t + 1)
                nc.scalar.copy(nwT.rearrange("p q n -> p (q n)"), bank[0][:, :]).then_inc(nw_out, 1)
                act.wait_ge(u_mm, t + 1)
                nc.scalar.copy(u_sb, bank[5][:, :]).then_inc(u_out, 1)

            def attention_norm(t):
                f(s_sq, tokp[:, SQ0:SV0], ACT.Square).then_inc(s_squares, 1)
                norm_root(norm_of(t, 1), s_rs)

            def piece8(t):
                act.wait_ge(s_T, t + 1)
                f(sqT.rearrange("p q n -> p (q n)"), bank[1][:, :], ACT.Copy, scale=q_gain[:, 0:1]).then_inc(s_T_out, 1)
                act.wait_ge(window_moved, t + 1)
                f(kwin[:, CHUNK:WIN], bank[2][:, 0:P], ACT.Copy, scale=k_gain[:, 0:1]).then_inc(s_T_out, 1)
                f(zs, tokp[:, Z0:Z0 + GW], ACT.Silu).then_inc(silu_z, 1)
                act.wait_ge(o_inter_mm, 2 * t + 2)
                for r in range(2):
                    nc.scalar.copy(o_inter.rearrange("p (q r d) -> p r q d", r=2, d=HD)[:, r],
                                        bank[3 + r][:, 0:256].rearrange("p (q d) -> p q d", d=HD)).then_inc(o_inter_out, 1)
                act.wait_ge(o_sum, t + 1)
                f(o_sq, o_sb, ACT.Square).then_inc(o_squares, 1)
                norm_root(norm_of(t, 2), o_rs)
                act.wait_ge(o_T, t + 1)
                nc.scalar.copy(mixT[:, 0:4, :].rearrange("p s n -> p (s n)"), bank[0][:, :]).then_inc(mix_ready, 1)

            def piece9(t):
                act.wait_ge(s_max, t + 1)
                for h in range(NH):
                    f(probs[:, h, CHUNK:256], probs[:, h, CHUNK:256], ACT.Exp, bias=s_nm[:, h:h + 1],
                      accum_out=s_den[:, h:h + 1])
                f(s_es, s_gap, ACT.Exp).then_inc(s_exp, 1)

            def piece10(t):
                for b in range(4):
                    act.wait_ge(probs_T, 4 * t + b + 1)
                    nc.scalar.copy(probsT[:, 4 * b:4 * b + 4, :].rearrange("p s n -> p (s n)"),
                                        bank[1 + b][:, :]).then_inc(probsT_ready, 1)

            def piece11(t):
                act.wait_ge(av_mm, t + 1)
                nc.scalar.copy(mixT[:, 4:8, :].rearrange("p s n -> p (s n)"), bank[5][:, :]).then_inc(mix_ready, 1)

            def piece12(t):
                act.wait_ge(h1_ready, 2 * t + 2)
                f(h_junk, h1, ACT.Square, accum_out=h_ss).then_inc(row_squares, 1)
                norm_root(norm_of(t, 3), h_rs)

            def normed_T(t):
                for i in range(2):
                    act.wait_ge(n2_T, 2 * t + i + 1)
                    nc.scalar.copy(n2T[:, 4 * i:4 * i + 4, :].rearrange("p s n -> p (s n)"), bank[2 + i][:, :]).then_inc(n2T_ready, 1)

            def query_pair(t, pair):
                for u in range(2):
                    act.wait_ge(query_mm, NQ * t + 2 * pair + u + 1)
                    nc.scalar.copy(qr[u], bank[4 - u][:, 0:QCOL]).then_inc(qr_ready, 1)
                for u in range(2):
                    act.wait_ge(qr_T, NQ * t + 2 * pair + u + 1)
                    nc.scalar.copy(qrT[u].rearrange("p s n -> p (s n)"),
                                   bank[(5, 2)[u]][:, 0:QCOL]).then_inc(qrT_ready, 1)
                for u in range(2):
                    act.wait_ge(score_mm, NQ * t + 2 * pair + u + 1)
                    at = 2 * (2 * pair + u)
                    nc.scalar.copy(scores[:, at:at + 2, :].rearrange("p s n -> p (s n)"),
                                   bank[u][:, 0:QCOL]).then_inc(scores_ready, 1)

            def piece_gate(t, cols=slice(0, SLOTS)):
                act.wait_ge(gate_arg, 1 if cols.stop == EARLY * G else t + 2)
                f(gate_new[:, cols], gate_new[:, cols], ACT.Exp).then_inc(gate_exp, 1)

            pieces = [lambda t: (piece0(t), piece1(t)), lambda t: (decays_of(t), piece2(t)),
                      lambda t: (piece3(t), level(t, 1)), lambda t: (level(t, 2), level(t, 3)),
                      lambda t: (level(t, 4), piece6(t)), attention_norm, piece8, piece9,
                      lambda t: (piece10(t), piece11(t)), piece12, lambda t: (normed_T(t), query_pair(t, 0)),
                      lambda t: query_pair(t, 1), lambda t: query_pair(t, 2), lambda t: query_pair(t, 3),
                      piece_gate, lambda t: None]
            assert len(pieces) == NG

            def experts(t, g):
                act.wait_ge(u_used, t * SLOTS + g * G + G)
                f(gel[:, g * G:g * G + G], hid[:, g * G:g * G + G], ACT.Gelu).then_inc(gelu, 1)
                act.wait_ge(weights_ready, t * NG + g + 1)
                for j in range(G):
                    if not (isinstance(t, int) and t == 0 and g == 0):
                        act.wait_ge(v_used, t * SLOTS + (g - 1) * G + j + 1)
                    f(diag[:, j, :], ident, ACT.Copy, scale=act_w[:, g * G + j:g * G + j + 1]).then_inc(diag_ready, 1)

            for piece in pieces[:10]:
                piece(0)
            normed_T(0)
            for pair in range(3):
                query_pair(0, pair)
            piece_gate(0, slice(0, EARLY * G))
            query_pair(0, 3)
            for g in range(FIRST):
                experts(0, g)
            piece_gate(0, slice(EARLY * G, SLOTS))
            for i, group in enumerate(merged(pieces)):
                experts(0, FIRST + i)
                for piece in group:
                    piece(1)
            with act.Fori(2, NT) as t:
                for g in range(NG):
                    experts(t - 1, g)
                    pieces[g](t)

            def gate_norm(k):
                if k == NT - 1:
                    act.wait_ge(h2_ready, 2 * NT)
                else:
                    act.wait_ge(rows_in[k % 2], ple_loaded(k))
                f(c_junk, ple_rows(k), ACT.Square, accum_out=c_ss).then_inc(row_squares, 1)
                act.wait_ge(mean_square, 5 * NT + k + 1)
                f(c_rs, c_rs, ACT.Sqrt).then_inc(root, 1)

            def gate_T(k):
                act.wait_ge(h1_mm, 2 * NT + 2 * k)
                for i in range(2):
                    act.wait_ge(n2_T, 2 * NT + 2 * k + i + 1)
                    nc.scalar.copy(c_nT[:, 4 * i:4 * i + 4, :].rearrange("p s n -> p (s n)"),
                                   bank[i][:, :]).then_inc(n2T_ready, 1)

            def gate_half(k, n):
                act.wait_ge(h1_mm, 2 * NT + 2 * k + n + 1)
                act.wait_ge(c_gated, k)
                f(c_e[:, n * 512:n * 512 + 512], bank[3 + n][:, :], ACT.Sigmoid).then_inc(c_gate, 1)

            act.wait_ge(vector_front, NT)
            for g in range(NG):
                experts(NT - 1, g)
                k = (g - 1) // 2
                if g == 0:
                    gate_norm(0)
                elif g == NG - 1:
                    pass
                elif g % 2:
                    gate_T(k)
                    gate_half(k, 0)
                else:
                    if k + 1 < NT - 1:
                        gate_norm(k + 1)
                    gate_half(k, 1)
            gate_norm(NT - 1)
            gate_T(NT - 1)
            for n in range(2):
                gate_half(NT - 1, n)

        @block.tensor
        def _(pe):
            def mm(out_, lhsT, rhs, start=True, stop=True, **kw):
                return nc.tensor.matmul(out_, lhsT, rhs, start=start, stop=stop, **kw)

            def turn(out_, in_):
                return nc.tensor.transpose(out_, in_, ident)

            pe.wait_ge(consts_loaded, 16)
            def turn_tile(t, u):
                pe.wait_ge(a_n_ready, t + u + 1)
                pe.wait_ge(a_nT_ready, (t + u) * 2)
                for c in range(DC):
                    last = turn(bank[c // 4][:, (c % 4) * P:(c % 4) * P + P], a_n[u][:, c * P:c * P + P])
                    if c % 4 == 3:
                        last.then_inc(a_turned, 1)

            def project_tile(t, u):
                first = isinstance(t, int) and t + u == 0
                pe.wait_ge(a_nT_ready, (t + u + 1) * 2)
                for n, width in enumerate((512, 512, TOKW - 1024)):
                    if first:
                        pe.wait_ge(a_w_loaded[n], 16)
                    else:
                        pe.wait_ge(a_tok_ready, (t + u - 1) * 3 + n + 1)
                    for c in range(DC):
                        last = mm(bank[2 + n][:, 0:width], a_nTt[u][:, c, :], a_w[:, c, n * 512:n * 512 + width],
                                  c == 0, c == DC - 1)
                    last.then_inc(a_tok_mm, 1)

            def token_pair(t, more=True):
                turn_tile(t, 1)
                project_tile(t, 0)
                if more:
                    turn_tile(t + 2, 0)
                project_tile(t, 1)

            turn_tile(0, 0)
            token_pair(0)
            with pe.Fori(1, NT // 2 - 1) as pair:
                token_pair(pair * 2)
            token_pair(NT - 2, False)

            pe.wait_ge(a_nT_copied, NT)
            pe.wait_ge(a_tok_ready, 3 * NT)

            def channels(ct, u):
                pe.wait_ge(wq_loaded[u], ct * 8 + 16)
                if not isinstance(ct, int):
                    pe.wait_ge(a_in_ready, (ct + u) * 2 - 2)
                for half in range(2):
                    for c in range(DC):
                        last = mm(bank[2 * u + half][:, :], a_wc[u][:, c, :], a_nT[:, c, half * 512:half * 512 + 512],
                                  c == 0, c == DC - 1)
                    last.then_inc(a_channels_mm, 1)

            for u in range(2):
                channels(0, u)
            pe.wait_ge(keys_loaded, 16)
            for b in range(4):
                if b >= 2:
                    pe.wait_ge(keysT_ready, b - 1)
                for i in range(4):
                    last = turn(bank[4 + b % 2][:, i * P:i * P + P], keys_in[:, 4 * b + i, :])
                last.then_inc(keys_T, 1)
            pe.wait_ge(params_b, 16 * 9)
            pe.wait_ge(keysT_ready, 4)
            for h in range(NH):
                if h >= 2:
                    pe.wait_ge(rel_rows_ready, h - 1)
                mm(bank[4 + h % 2][:, 0:RELS], rel_sb[:, h:h + 1].broadcast_to([REL_BUCKETS, P]),
                   cst[0:REL_BUCKETS, C_REL:C_REL + RELS]).then_inc(rel_mm, 1)
            with pe.Fori(1, QKV // P // 2) as pair:
                ct = pair * 2
                for u in range(2):
                    channels(ct, u)

            pe.wait_ge(a_in_ready, QKV // P * 2)

            def piece0(t):
                pe.wait_ge(vector_front, t)
                pe.wait_ge(qkv_loaded, (t + 1) * 16)
                for c in range(QKV // P):
                    last = turn(bank[c // 4][:, (c % 4) * P:(c % 4) * P + P], qkv_in[:, c, :])
                    if c % 4 == 3:
                        last.then_inc(qkv_tok, 1)

            def piece1(t):
                pe.wait_ge(g_ready, t + 1)
                for i, at in enumerate((C_TRIL, C_BLOCK, C_CH0, C_CH1)):
                    last = mm(bank[3][:, 8 * i:8 * i + 8], cst[:, at:at + P], gl)
                last.then_inc(cumsum, 1)
                for r in range(2):
                    pe.wait_ge(gdiag_ready, 2 * t + r + 1)
                    mm(bank[4 + r][:, :], cst[:, C_ONES:C_ONES + P],
                            gdiag[:, 4 * r:4 * r + 4, :].rearrange("p s n -> p (s n)")).then_inc(gc_rows, 1)

            def piece2(t):
                for i, (src, b) in enumerate(((kn, 3), (nkb, 4), (qn, 5), (qg, 0))):
                    pe.wait_ge(scaled, 7 * t + i + 1)
                    for q in range(4):
                        last = turn(bank[b][:, q * P:q * P + P], src[:, q * P:q * P + P])
                    last.then_inc(heads_T, 1)

            def turn_inverse(t, n):
                for r in range(2):
                    pe.wait_ge(invT_ready, 12 * t + n + r + 1)
                    for q in range(4):
                        last = turn(bank[(0, 5)[r]][:, q * P:q * P + P], invT[:, 4 * r + q, :])
                    last.then_inc(inv_turned, 1)

            def piece3(t):
                pe.wait_ge(scaled, 7 * t + 7)
                pe.wait_ge(heads_T_out, 4 * t + 2)
                for r in range(2):
                    for q in range(4):
                        last = mm(bank[1 + r][:, q * P:q * P + P], knT[r * HD:r * HD + HD, q, :], nkbT[r * HD:r * HD + HD, q, :])
                    last.then_inc(kk_mm, 1)
                pe.wait_ge(heads_T_out, 4 * t + 3)
                for r in range(2):
                    for q in range(4):
                        last = mm(bank[3 + r][:, q * P:q * P + P], knT[r * HD:r * HD + HD, q, :], qnT[r * HD:r * HD + HD, q, :])
                    last.then_inc(qk_mm, 1)
                pe.wait_ge(heads_T_out, 4 * t + 4)
                turn_inverse(t, 0)

            def level(t, l):
                n = 10 * t + 2 * (l - 1)
                for r in range(2):
                    pe.wait_ge(inv_ready, n + r + 1)
                    for q in range(4):
                        last = mm(bank[1 + r][:, q * P:q * P + P], amT[:, 4 * r + q, :], inv[:, 4 * r + q, :])
                    last.then_inc(level_x, 1)
                for r in range(2):
                    pe.wait_ge(level_x_out, n + r + 1)
                    for q in range(4):
                        last = mm(bank[3 + r][:, q * P:q * P + P], step_x[:, 4 * r + q, :], invT[:, 4 * r + q, :])
                    last.then_inc(level_p, 1)
                if l < LEVELS - 1:
                    turn_inverse(t, 2 * l)

            def piece6(t):
                level(t, 5)
                pe.wait_ge(invT_ready, 12 * t + 12)
                for q in range(4):
                    for r in range(2):
                        h, s = 2 * q + r, 4 * r + q
                        last = mm(bank[0][r * HD:r * HD + HD, q * P:q * P + P], nkbg[:, h * HD:h * HD + HD], invT[:, s, :])
                last.then_inc(nw_mm, 1)
                for h in range(NH):
                    last = mm(bank[5][:, h * HD:h * HD + HD], invT[:, 4 * (h % 2) + h // 2, :], vb[:, h * HD:h * HD + HD])
                last.then_inc(u_mm, 1)

            def piece7(t, c):
                rows = slice(c * CHUNK, c * CHUNK + CHUNK)
                pe.wait_ge(nw_out, t + 1)
                pe.sem_inc(wait_carrier)
                pe.wait_ge(state_ready, 2 * t + c + 1)
                pe.sem_inc(wait_carrier)
                for r in range(2):
                    chans = slice(r * HD, r * HD + HD)
                    for q in range(4):
                        last = mm(bank[1 + r][rows, q * HD:q * HD + HD], nwT[chans, q, rows], state[chans, q, :])
                last.then_inc(ws_mm, 1)
                for r in range(2):
                    chans = slice(r * HD, r * HD + HD)
                    for q in range(4):
                        last = mm(bank[3 + r][rows, q * HD:q * HD + HD], qgT[chans, q, rows], state[chans, q, :])
                last.then_inc(o_inter_mm, 1)
                pe.wait_ge(v_new_ready, 4 * t + 2 * c + 2)
                pe.sem_inc(wait_carrier)
                for h in range(NH):
                    r, q = h % 2, h // 2
                    last = mm(bank[0][r * HD:r * HD + HD, q * HD:q * HD + HD], kdec[rows, h * HD:h * HD + HD],
                              v_new[rows, h * HD:h * HD + HD])
                last.then_inc(kv_mm, 1)

            def piece8(t):
                pe.wait_ge(s_normed, 2 * t + 2)
                for q in range(4):
                    turn(bank[1][:, q * P:q * P + P], s_n[:, q * P:q * P + P])
                turn(bank[2][:, 0:P], s_n[:, GW:GW + P]).then_inc(s_T, 1)
                for h in range(NH):
                    last = mm(bank[5][:, h * HD:h * HD + HD], qkT[:, 4 * (h % 2) + h // 2, :], v_new[:, h * HD:h * HD + HD])
                last.then_inc(o_intra_mm, 1)
                pe.wait_ge(state_ready, 2 * t + 3)
                pe.wait_ge(o_normed, t + 1)
                for q in range(4):
                    last = turn(bank[0][:, q * P:q * P + P], o_sb[:, q * P:q * P + P])
                last.then_inc(o_T, 1)

            def piece9(t):
                pe.wait_ge(s_T_out, 2 * t + 2)
                pe.wait_ge(mix_ready, 2 * t + 1)
                for h in range(NH):
                    kv, g = h // 4, h % 4
                    chans = slice(kv * HD, kv * HD + HD)
                    last = mm(bank[bias_banks[h // 2]][:, (h % 2) * WIN:(h % 2) * WIN + WIN], sqT[chans, g, :],
                              kwin[chans, :])
                    if h % 2:
                        last.then_inc(logits_mm, 1)

            def piece10(t):
                pe.wait_ge(probs_ready, t + 1)
                for i in range(16):
                    last = turn(bank[1 + i // 4][:, (i % 4) * P:(i % 4) * P + P], probs[:, i // 2, (i % 2) * P:(i % 2) * P + P])
                    if i % 4 == 3:
                        last.then_inc(probs_T, 1)

            def piece11(t):
                pe.wait_ge(probsT_ready, 4 * t + 4)
                for h in range(NH):
                    kv = h // 4
                    to = bank[5][(h % 2) * HD:(h % 2) * HD + HD, (h // 2) * P:(h // 2) * P + P]
                    mm(to, vprev[:, kv * HD:kv * HD + HD], probsT[:, 2 * h, :], True, False)
                    last = mm(to, vcur[:, kv * HD:kv * HD + HD], probsT[:, 2 * h + 1, :], False, True)
                last.then_inc(av_mm, 1)
                pe.wait_ge(mix_ready, 2 * t + 2)
                pe.wait_ge(w_out_loaded, 32)
                project_out(0)

            def project_out(n):
                for c in range(DC):
                    last = mm(bank[n][:, :], mixT[:, c, :], w_out_sb[:, c, n * 512:n * 512 + 512], c == 0, c == DC - 1)
                last.then_inc(h1_mm, 1)

            def piece12(t):
                pe.wait_ge(xb_ready, t + 1)
                for c in range(DC):
                    last = turn(bank[2 + c // 4][:, (c % 4) * P:(c % 4) * P + P], xb_new[:, c * P:c * P + P])
                    if c % 4 == 3:
                        last.then_inc(n2_T, 1)
                pe.wait_ge(n2T_ready, 2 * t + 2)

            def query_pair(t, pair):
                n = NQ * t + 2 * pair
                for u in range(2):
                    pe.wait_ge(wq_loaded[u], 8 * (QKV // P) + 16 * (NQ // 2) * t + 16 * pair + 16)
                    for c in range(DC):
                        last = mm(bank[4 - u][:, 0:QCOL], n2T[:, c, :], wq[u][:, c, :], c == 0, c == DC - 1)
                    last.then_inc(query_mm, 1)
                for u in range(2):
                    pe.wait_ge(qr_ready, n + u + 1)
                    for s in range(2):
                        last = turn(bank[(5, 2)[u]][:, s * P:s * P + P], qr[u][:, s * P:s * P + P])
                    last.then_inc(qr_T, 1)
                for u in range(2):
                    pe.wait_ge(qrT_ready, n + u + 1)
                    pe.wait_ge(scores_ready, n - 1 + u if pair else NQ * t)
                    for s in range(2):
                        last = mm(bank[u][:, s * P:s * P + P], qrT[u][:, s, :], keysT[:, 2 * (2 * pair + u) + s, :])
                    last.then_inc(score_mm, 1)

            pieces = [piece0, lambda t: (piece1(t), piece2(t)), lambda t: (piece3(t), level(t, 1)),
                      lambda t: (level(t, 2), level(t, 3)), lambda t: (level(t, 4), piece6(t)),
                      lambda t: (piece7(t, 0), piece7(t, 1)), piece8, piece9, lambda t: (piece10(t), piece11(t)),
                      lambda t: project_out(1), lambda t: (piece12(t), query_pair(t, 0)),
                      lambda t: query_pair(t, 1), lambda t: query_pair(t, 2), lambda t: query_pair(t, 3),
                      lambda t: None, lambda t: None]

            def experts(t, g):
                if g == 0:
                    pe.wait_ge(h2_ready, t * 2)
                    for n in range(2):
                        last = mm(acc[:, n * 512:n * 512 + 512], ident, h1[:, n * 512:n * 512 + 512], True, False)
                    last.then_inc(h1_added, 1)
                for j in range(G):
                    pe.wait_ge(v_landed[j], (t * NG + g + 1) * 16)
                    pe.wait_ge(diag_ready, t * SLOTS + g * G + j + 1)
                    for n in range(2):
                        last = mm(acc[:, n * 512:n * 512 + 512], diag[:, j, :], v_ring[:, j, n * 512:n * 512 + 512],
                                  False, g == NG - 1 and j == G - 1)
                    last.then_inc(v_used, 1)

            def tile(t):
                for g in range(NG):
                    if g:
                        experts(t - 1, g - 1)
                    pieces[g](t)
                experts(t - 1, NG - 1)

            pe.wait_ge(rel_rows_ready, NH)
            for piece in pieces:
                piece(0)
            for g in range(FIRST - 1):
                experts(0, g)
            for i, group in enumerate(merged(pieces)):
                experts(0, FIRST - 1 + i)
                for piece in group:
                    piece(1)
            experts(0, NG - 1)
            with pe.Fori(2, NT) as t:
                tile(t)

            def turn_p(k):
                pe.wait_ge(rows_in[k % 2], ple_loaded(k))
                pe.wait_ge(c_gated, k)
                for c in range(PLE // P):
                    last = turn(bank[2][:, c * P:c * P + P], c_p[k % 2][:, c * P:c * P + P])
                last.then_inc(c_pT_turned, 1)

            def turn_rows(k):
                pe.wait_ge(xb_ready, NT + k + 1)
                pe.wait_ge(n2T_ready, 2 * NT + 2 * k)
                for c in range(DC):
                    last = turn(bank[c // 4][:, (c % 4) * P:(c % 4) * P + P], c_n[:, c * P:c * P + P])
                    if c % 4 == 3:
                        last.then_inc(n2_T, 1)

            def gate(k, n):
                pe.wait_ge(n2T_ready, 2 * NT + 2 * k + 2)
                if k:
                    pe.wait_ge(c_gate, 2 * (k - 1) + n + 1)
                for c in range(DC):
                    last = mm(bank[3 + n][:, :], c_nT[:, c, :], wg_sb[:, c, n * 512:n * 512 + 512], c == 0, c == DC - 1)
                last.then_inc(h1_mm, 1)

            def project_p(k, n):
                pe.wait_ge(c_pT_ready, k + 1)
                for c in range(PLE // P):
                    last = mm(bank[(5, 2)[n]][:, :], c_pT[:, c, :], wp_sb[:, c, n * 512:n * 512 + 512],
                              c == 0, c == PLE // P - 1)
                last.then_inc(c_proj_mm, 1)

            pe.wait_ge(vector_front, NT)
            for g in range(NG):
                if g:
                    experts(NT - 1, g - 1)
                if g == 1:
                    pe.wait_ge(c_w_loaded, 32)
                k = (g - 1) // 2
                if g == NG - 1:
                    turn_p(NT - 1)
                elif g % 2:
                    turn_p(k)
                    turn_rows(k)
                    gate(k, 0)
                elif g:
                    project_p(k, 0)
                    project_p(k, 1)
                    gate(k, 1)
            experts(NT - 1, NG - 1)
            for n in range(2):
                project_p(NT - 1, n)
            turn_rows(NT - 1)
            for n in range(2):
                gate(NT - 1, n)

        @block.vector
        def _(dve):
            v = nc.vector
            counted = [0]

            def steps(t):
                counted[0] += 1
                return t * V_STEPS + counted[0] + (0 if isinstance(t, int) and t == 0 else V_FIRST)

            def mean_to_ms(out_, in_, n):
                return v.tensor_scalar(out_, in_, 1.0 / n, EPS, ALU.mult, ALU.add)

            for u in range(2):
                last = v.memset(a_in[u][:, 0:CONV - 1], 0.0)
            last.then_inc(a_halo_zero, 1)
            dve.wait_ge(g_mix_loaded, 16)
            with dve.Fori(0, NT // 2) as pair:
                t = pair * 2
                for u in range(2):
                    dve.wait_ge(row_squares, t + u + 1)
                    mean_to_ms(a_rs[:, u:u + 1], a_ss[:, u:u + 1], D).then_inc(mean_square, 1)
                    dve.wait_ge(root, t + u + 1)
                    v.reciprocal(a_rs[:, u:u + 1], a_rs[:, u:u + 1]).then_inc(inverse_root, 1)
                    dve.wait_ge(inverse_root, t + u + 1)
                    v.tensor_scalar(a_n[u][:], a_x[u][:], a_rs[:, u:u + 1], None, ALU.mult).then_inc(a_n_ready, 1)
                    for i in range(2):
                        dve.wait_ge(a_turned, (t + u) * 2 + i + 1)
                        v.tensor_tensor(a_nTt[u][:, 4 * i:4 * i + 4, :], bank[i][:, :].rearrange("p (c n) -> p c n", n=P),
                                             per_head(g_mix_c[:, 4 * i:4 * i + 4], 4, P), ALU.mult).then_inc(a_nT_ready, 1)
            dve.wait_ge(taps_loaded, 16 * CONV)
            with dve.Fori(0, QKV // P // 2) as pair:
                ct = pair * 2
                for u in range(2):
                    dve.wait_ge(a_in_ready, (ct + u + 1) * 2)
                    for k in range(CONV):
                        tap = conv_c[:, k, bass.ds(ct + u, 1)]
                        if k == 0:
                            ins = v.tensor_scalar(a_cv[u][:], a_in[u][:, k:k + SEQ], tap, None, ALU.mult)
                        else:
                            dve.wait_ge(a_conv_sum, (ct + u) * CONV + k)
                            ins = v.scalar_tensor_tensor(a_cv[u][:], a_in[u][:, k:k + SEQ], tap, a_cv[u][:], ALU.mult, ALU.add)
                        ins.then_inc(a_conv_sum, 1)

            dve.wait_ge(a_tok_mm, 3 * NT)
            v.memset(kwin[:], 0.0)
            v.memset(vcur[:], 0.0)
            v.memset(v_new, 0.0)
            v.memset(state[:], 0.0).then_inc(state_ready, 1)
            dve.wait_ge(rate_exp, 1)
            v.tensor_scalar(neg_rate[:], neg_rate[:], -1.0, None, ALU.mult).then_inc(rate_ready, 1)
            dve.wait_ge(rate_ready, 1)
            dve.wait_ge(bias_loaded, 16)
            v.tensor_tensor(bias_t[:], bias_t[:], cst[:, C_WIN:C_WIN + WIN].unsqueeze(1).broadcast_to([P, NH, WIN]),
                                 ALU.add).then_inc(bias_ready, 1)
            dve.wait_ge(bias_ready, 1)
            dve.wait_ge(state_ready, 1)
            dve.wait_ge(w_out_loaded, 32)

            def gc_of(r, width=P):
                return gcs[:, 0:NH].rearrange("p (q r) -> p r q", r=2)[:, r].unsqueeze(2).broadcast_to([P, 4, width])

            def piece0(t):
                dve.wait_ge(vector_front, t)
                dve.wait_ge(squares, 2 * t + 2)
                v.reduce_sum(ssq, square.rearrange("p (h d) -> p h d", d=HD), AX.X).then_inc(vector_step, 1)
                dve.wait_ge(vector_step, steps(t))
                v.tensor_scalar(rst, ssq, EPS, None, ALU.add).then_inc(mean_square, 1)
                dve.wait_ge(root, norm_of(t, 0) + 1)
                v.reciprocal(rst, rst).then_inc(vector_step, 1)
                dve.wait_ge(vector_step, steps(t))
                v.tensor_scalar(rst[:, 0:NH], rst[:, 0:NH], HD ** -0.5, None, ALU.mult).then_inc(vector_step, 1)
                dve.wait_ge(vector_step, steps(t))

            def piece1(t):
                dve.wait_ge(tok_loaded, (t + 1) * 16)
                v.tensor_tensor(xa, tokp[:, A0:A0 + NH], dt_row[:], ALU.add).then_inc(vector_step, 1)
                dve.wait_ge(vector_step, steps(t))
                v.scalar_tensor_tensor(xabs, xa, -1.0, xa, ALU.mult, ALU.max).then_inc(x_abs, 1)
                dve.wait_ge(beta_exp, t + 1)
                v.tensor_scalar(eb, eb, 1.0, None, ALU.add).then_inc(vector_step, 1)
                dve.wait_ge(vector_step, steps(t))
                v.reciprocal(beta, eb).then_inc(vector_step, 1)
                dve.wait_ge(vector_step, steps(t))
                v.tensor_scalar(nbeta, beta, -1.0, None, ALU.mult).then_inc(vector_step, 1)
                dve.wait_ge(vector_step, steps(t))
                dve.wait_ge(softplus_tail, t + 1)
                v.scalar_tensor_tensor(gl, xa, 0.0, spl, ALU.max, ALU.add).then_inc(vector_step, 1)
                dve.wait_ge(vector_step, steps(t))
                v.tensor_tensor(gl, gl, neg_rate[:], ALU.mult).then_inc(g_ready, 1)

            def decays_of(t):
                dve.wait_ge(cumsum, t + 1)
                v.tensor_copy(gcs, bank[3][:, 0:32]).then_inc(gcs_ready, 1)
                dve.wait_ge(gcs_ready, t + 1)
                v.tensor_tensor(kgap, gcs[:, NH:2 * NH], gcs[:, 0:NH], ALU.subtract).then_inc(k_gap, 1)
                for r in range(2):
                    v.tensor_tensor(gdiag[:, 4 * r:4 * r + 4, :], ident.unsqueeze(1).broadcast_to([P, 4, P]), gc_of(r),
                                         ALU.mult).then_inc(gdiag_ready, 1)
                for r in range(2):
                    dve.wait_ge(gc_rows, 2 * t + r + 1)
                    last = v.tensor_tensor(decT[:, 4 * r:4 * r + 4, :], bank[4 + r][:, :].rearrange("p (s n) -> p s n", n=P),
                                           gc_of(r), ALU.subtract)
                last.then_inc(vector_step, 1)
                dve.wait_ge(vector_step, steps(t))
                v.tensor_scalar(decT, decT, 0.0, None, ALU.min).then_inc(dec_arg, 1)
                dve.wait_ge(dec_exp, t + 1)
                v.tensor_tensor(decT, decT, cst[:, C_TRIL:C_TRIL + P].unsqueeze(1).broadcast_to([P, 8, P]), ALU.mult).then_inc(vector_step, 1)
                dve.wait_ge(vector_step, steps(t))

            def piece2(t):
                dve.wait_ge(qkv_tok, 3 * t + 3)
                dve.wait_ge(h1_added, t)
                dve.wait_ge(decays, t + 1)
                n = 7 * t
                for i, (dst, src, factor, need) in enumerate((
                        (kn, bank[1][:, :], rst[:, NH:2 * NH], 0), (nkb, kn, nbeta, 1), (qn, bank[0][:, :], rst[:, 0:NH], 0),
                        (qg, qn, eg, 3), (nkbg, nkb, eg, 2), (vb, bank[2][:, :], beta, 0), (kdec, kn, kd, 1))):
                    if need:
                        dve.wait_ge(scaled, n + need)
                    v.tensor_tensor(heads(dst), heads(src), per_head(factor), ALU.mult).then_inc(scaled, 1)

            def level_mask(l):
                return cst[:, C_LEVEL + l * P:C_LEVEL + l * P + P].bitcast(U32).unsqueeze(1).broadcast_to([P, 4, P])

            def piece3(t):
                for r in range(2):
                    dve.wait_ge(kk_mm, 2 * t + r + 1)
                    last = v.tensor_tensor(amT[:, 4 * r:4 * r + 4, :], bank[1 + r][:, :].rearrange("p (s n) -> p s n", n=P),
                                           decT[:, 4 * r:4 * r + 4, :], ALU.mult)
                dve.wait_ge(heads_T, 4 * t + 4)
                v.tensor_copy(invT, ident.unsqueeze(1).broadcast_to([P, 8, P])).then_inc(vector_step, 1)
                dve.wait_ge(vector_step, steps(t))
                dve.sem_inc(wait_carrier)
                for r in range(2):
                    v.copy_predicated(invT[:, 4 * r:4 * r + 4, :], level_mask(0), amT[:, 4 * r:4 * r + 4, :]).then_inc(invT_ready, 1)
                for r in range(2):
                    dve.wait_ge(qk_mm, 2 * t + r + 1)
                    v.tensor_tensor(qkT[:, 4 * r:4 * r + 4, :], bank[3 + r][:, :].rearrange("p (s n) -> p s n", n=P),
                                         decT[:, 4 * r:4 * r + 4, :], ALU.mult).then_inc(qkT_ready, 1)

            def level(t, l):
                for r in range(2):
                    dve.wait_ge(level_p, 10 * t + 2 * (l - 1) + r + 1)
                    dve.sem_inc(wait_carrier)
                    v.copy_predicated(invT[:, 4 * r:4 * r + 4, :], level_mask(l),
                                           bank[3 + r][:, :].rearrange("p (s n) -> p s n", n=P)).then_inc(invT_ready, 1)

            def piece7(t, c):
                rows = slice(c * CHUNK, c * CHUNK + CHUNK)
                dve.wait_ge(u_out, t + 1)
                dve.wait_ge(ws_mm, 2 * t + c + 1)
                by_r = lambda ap: ap[rows, :].rearrange("p (q r d) -> p r q d", r=2, d=HD)
                for r in range(2):
                    v.tensor_tensor(by_r(v_new)[:, r], by_r(u_sb)[:, r],
                                         bank[1 + r][rows, 0:256].rearrange("p (q d) -> p q d", d=HD), ALU.add).then_inc(v_new_ready, 1)
                dve.wait_ge(kv_mm, 2 * t + c + 1)
                v.tensor_tensor(state[:], state[:], per_head(glp[:, c, :], 4), ALU.mult).then_inc(vector_step, 1)
                dve.wait_ge(vector_step, steps(t))
                v.tensor_tensor(state[:], state[:], bank[0][:, 0:256].rearrange("p (q d) -> p q d", d=HD), ALU.add).then_inc(state_ready, 1)

            def attention_norm(t):
                v.tensor_copy(kwin[:, 0:CHUNK], kwin[:, P:WIN]).then_inc(vector_step, 1)
                dve.wait_ge(vector_step, steps(t))
                v.tensor_copy(vprev[:], vcur[:]).then_inc(vector_step, 1)
                dve.wait_ge(vector_step, steps(t))
                v.tensor_copy(vcur[:], tokp[:, SV0:SV0 + P]).then_inc(window_moved, 1)
                dve.wait_ge(s_squares, t + 1)
                v.reduce_sum(s_ss, heads(s_sq, 10), AX.X).then_inc(vector_step, 1)
                dve.wait_ge(vector_step, steps(t))
                mean_to_ms(s_rs, s_ss, HD).then_inc(mean_square, 1)
                dve.wait_ge(root, norm_of(t, 1) + 1)
                v.reciprocal(s_rs, s_rs).then_inc(vector_step, 1)
                dve.wait_ge(vector_step, steps(t))
                v.tensor_scalar(s_rs[:, 0:NH], s_rs[:, 0:NH], HD ** -0.5, None, ALU.mult).then_inc(vector_step, 1)
                dve.wait_ge(vector_step, steps(t))
                v.tensor_tensor(s_n[:, 0:GW].rearrange("p (g k d) -> p k g d", k=NKV, d=HD),
                                     tokp[:, SQ0:SK0].rearrange("p (k g d) -> p k g d", k=NKV, d=HD),
                                     s_rs[:, 0:NH].rearrange("p (k g) -> p k g", k=NKV).unsqueeze(3).broadcast_to([P, NKV, 4, HD]),
                                     ALU.mult).then_inc(s_normed, 1)
                v.tensor_tensor(heads(s_n[:, GW:GW + P], 2), heads(tokp[:, SK0:SV0], 2), per_head(s_rs[:, NH:10], 2),
                                     ALU.mult).then_inc(s_normed, 1)

            def piece8(t):
                dve.wait_ge(silu_z, t + 1)
                v.tensor_tensor(heads(zs), heads(zs), norm_g[:].unsqueeze(1).broadcast_to([P, NH, HD]), ALU.mult).then_inc(vector_step, 1)
                dve.wait_ge(vector_step, steps(t))
                dve.wait_ge(o_inter_out, 2 * t + 2)
                dve.wait_ge(o_intra_mm, t + 1)
                v.tensor_tensor(o_sb, o_inter, bank[5][:, :], ALU.add).then_inc(o_sum, 1)
                dve.wait_ge(o_squares, t + 1)
                v.reduce_sum(o_ss, heads(o_sq), AX.X).then_inc(vector_step, 1)
                dve.wait_ge(vector_step, steps(t))
                mean_to_ms(o_rs, o_ss, HD).then_inc(mean_square, 1)
                dve.wait_ge(root, norm_of(t, 2) + 1)
                v.reciprocal(o_rs, o_rs).then_inc(vector_step, 1)
                dve.wait_ge(vector_step, steps(t))
                v.tensor_tensor(heads(o_sb), heads(o_sb), per_head(o_rs), ALU.mult).then_inc(vector_step, 1)
                dve.wait_ge(vector_step, steps(t))
                v.tensor_tensor(o_sb, o_sb, zs, ALU.mult).then_inc(o_normed, 1)

            def piece9(t):
                v.memset(probs[:, :, 0:CHUNK], 0.0)
                for b in range(4):
                    dve.wait_ge(logits_mm, 4 * t + b + 1)
                    last = v.tensor_tensor(probs[:, 2 * b:2 * b + 2, CHUNK:256],
                                           bank[bias_banks[b]][:, 0:2 * WIN].rearrange("p (h w) -> p h w", h=2),
                                           bias_t[:, 2 * b:2 * b + 2, :], ALU.add)
                last.then_inc(vector_step, 1)
                dve.wait_ge(vector_step, steps(t))
                if isinstance(t, int) and t == 0:
                    last = v.memset(probs[:, :, CHUNK:2 * CHUNK], MASKED)
                else:
                    last = v.tensor_scalar(s_gap, sinks[:], 0.0, None, ALU.add)
                last.then_inc(vector_step, 1)
                dve.wait_ge(vector_step, steps(t))
                v.tensor_reduce(s_m, probs[:, :, CHUNK:256], AX.X, ALU.max).then_inc(vector_step, 1)
                dve.wait_ge(vector_step, steps(t))
                v.tensor_tensor(s_m, s_m, sinks[:], ALU.max).then_inc(vector_step, 1)
                dve.wait_ge(vector_step, steps(t))
                v.tensor_scalar(s_nm, s_m, -1.0, None, ALU.mult).then_inc(vector_step, 1)
                dve.wait_ge(vector_step, steps(t))
                v.tensor_tensor(s_gap, sinks[:], s_nm, ALU.add).then_inc(s_max, 1)

            def piece10(t):
                dve.wait_ge(s_exp, t + 1)
                v.tensor_tensor(s_den, s_den, s_es, ALU.add).then_inc(vector_step, 1)
                dve.wait_ge(vector_step, steps(t))
                v.reciprocal(s_den, s_den).then_inc(vector_step, 1)
                dve.wait_ge(vector_step, steps(t))
                v.tensor_tensor(probs[:, :, CHUNK:256], probs[:, :, CHUNK:256], per_head(s_den, NH, WIN), ALU.mult).then_inc(probs_ready, 1)

            def residual(t, n):
                dve.wait_ge(x_loaded, (t + 1) * 16)
                dve.wait_ge(h1_mm, 2 * t + n + 1)
                v.tensor_tensor(h1[:, n * 512:n * 512 + 512], x_t[:, n * 512:n * 512 + 512], bank[n][:, :],
                                ALU.add).then_inc(h1_ready, 1)

            def piece12(t):
                dve.wait_ge(row_squares, NT + t + 1)
                mean_to_ms(h_rs, h_ss, D).then_inc(mean_square, 1)
                dve.wait_ge(root, norm_of(t, 3) + 1)
                v.reciprocal(h_rs, h_rs).then_inc(vector_step, 1)
                dve.wait_ge(vector_step, steps(t))
                if not isinstance(t, int) or t >= 2:
                    dve.wait_ge(h2_stored, (t - 1) * 16)
                v.scalar_tensor_tensor(xb_new[:], h1, h_rs, g_ffn_b[:], ALU.mult, ALU.mult).then_inc(xb_ready, 1)

            def top16(t, values, tops, indices):
                first = slice(0, 8)
                second = slice(8, 16)
                for row, top, _ in zip(values, tops, indices):
                    last = v.max(top[:, first], row)
                last.then_inc(vector_step, 1)
                dve.wait_ge(vector_step, steps(t))
                dve.sem_inc(wait_carrier)
                for row, top, index in zip(values, tops, indices):
                    last = v.max_index(index[:, first], top[:, first], row)
                last.then_inc(vector_step, 1)
                dve.wait_ge(vector_step, steps(t))
                dve.sem_inc(wait_carrier)
                for row, top, _ in zip(values, tops, indices):
                    last = v.match_replace(row, top[:, first], row, LEAST)
                last.then_inc(vector_step, 1)
                dve.wait_ge(vector_step, steps(t))
                dve.sem_inc(wait_carrier)
                for row, top, _ in zip(values, tops, indices):
                    last = v.max(top[:, second], row)
                last.then_inc(vector_step, 1)
                dve.wait_ge(vector_step, steps(t))
                dve.sem_inc(wait_carrier)
                for row, top, index in zip(values, tops, indices):
                    last = v.max_index(index[:, second], top[:, second], row)
                last.then_inc(vector_step, 1)
                dve.wait_ge(vector_step, steps(t))

            def best_pair(t, pair):
                dve.wait_ge(scores_ready, NQ * t + 2 * pair + 2)
                dve.sem_inc(wait_carrier)
                halves = range(4 * pair, 4 * pair + 4)
                top16(t, [scores[:, s, :] for s in halves], [vtop[:, s, :] for s in halves], [itop[:, s, :] for s in halves])
                both = range(2 * pair, 2 * pair + 2)
                for i in both:
                    last = v.tensor_tensor(cand[:, i, :].rearrange("p (a b) -> p a b", b=TOPK),
                                           vtop[:, 2 * i, :].unsqueeze(2).broadcast_to([P, TOPK, TOPK]),
                                           vtop[:, 2 * i + 1, :].unsqueeze(1).broadcast_to([P, TOPK, TOPK]), ALU.add)
                last.then_inc(vector_step, 1)
                dve.wait_ge(vector_step, steps(t))
                dve.sem_inc(wait_carrier)
                top16(t, [cand[:, i, :] for i in both], [ctop[:, i, :] for i in both], [cidx[:, i, :] for i in both])

            def pick(t, h0, nh):
                hs, cols = slice(h0, h0 + nh), slice(h0 * TOPK, (h0 + nh) * TOPK)
                key_numbers = itop_f[:, 2 * h0:2 * (h0 + nh), :]
                v.tensor_copy(key_numbers, itop[:, 2 * h0:2 * (h0 + nh), :]).then_inc(vector_step, 1)
                dve.wait_ge(vector_step, steps(t))
                for half in range(2):
                    if half == 0:
                        ins = v.tensor_scalar(chalf[:, hs, :], cidx[:, hs, :], 4, None, ALU.logical_shift_right)
                    else:
                        ins = v.tensor_scalar(chalf[:, hs, :], cidx[:, hs, :], TOPK - 1, None, ALU.bitwise_and)
                    ins.then_inc(vector_step, 1)
                    dve.wait_ge(vector_step, steps(t))
                    v.tensor_copy(chalf_f[:, half, cols], chalf[:, hs, :].rearrange("p h k -> p (h k)")).then_inc(vector_step, 1)
                    dve.wait_ge(vector_step, steps(t))
                    v.tensor_tensor(onehot[:, hs].rearrange("p h k a -> p (h k) a"),
                                    cst[:, C_IOTA:C_IOTA + TOPK].unsqueeze(1).broadcast_to([P, nh * TOPK, TOPK]),
                                    chalf_f[:, half, cols].unsqueeze(2).broadcast_to([P, nh * TOPK, TOPK]),
                                    ALU.is_equal).then_inc(vector_step, 1)
                    dve.wait_ge(vector_step, steps(t))
                    by_half = key_numbers.rearrange("p (h f) k -> p f h k", f=2)[:, half]
                    v.tensor_tensor(onehot[:, hs], onehot[:, hs], by_half.unsqueeze(2).broadcast_to([P, nh, TOPK, TOPK]),
                                    ALU.mult).then_inc(vector_step, 1)
                    dve.wait_ge(vector_step, steps(t))
                    v.reduce_sum(e_half[:, half, cols], onehot[:, hs].rearrange("p h k a -> p (h k) a"),
                                 AX.X).then_inc(vector_step, 1)
                    dve.wait_ge(vector_step, steps(t))
                dve.wait_ge(ids_taken, t)
                ins = v.scalar_tensor_tensor(eid_new[:, cols], e_half[:, 0, cols], float(NKEYS), e_half[:, 1, cols],
                                             ALU.mult, ALU.add)
                ins.then_inc(first_ids_ready if h0 == 0 else vector_step, 1)
                if h0:
                    dve.wait_ge(vector_step, steps(t))

            def gates(t, h0, h1, signal_done):
                by_head = gate_new[:, h0 * TOPK:h1 * TOPK].rearrange("p (h k) -> p h k", k=TOPK)
                v.tensor_tensor(by_head, ctop[:, h0:h1, :], ctop[:, h0:h1, 0:1].broadcast_to([P, h1 - h0, TOPK]),
                                ALU.subtract).then_inc(gate_arg, 1)
                dve.wait_ge(gate_exp, 1 if h1 == 2 else t + 2)
                v.reduce_sum(g_sum[:, h0:h1], by_head, AX.X).then_inc(vector_step, 1)
                dve.wait_ge(vector_step, steps(t))
                v.reciprocal(g_inv[:, h0:h1], g_sum[:, h0:h1]).then_inc(vector_step, 1)
                dve.wait_ge(vector_step, steps(t))
                v.tensor_tensor(by_head, by_head, per_head(g_inv[:, h0:h1], h1 - h0, TOPK), ALU.mult).then_inc(signal_done, 1)

            def end_of_front():
                assert counted[0] == V_STEPS, counted
                counted[0] = 0

            pieces = [lambda t: (piece0(t), piece1(t)), lambda t: (decays_of(t), piece2(t)),
                      lambda t: (piece3(t), level(t, 1)), lambda t: (level(t, 2), level(t, 3)),
                      lambda t: (level(t, 4), level(t, 5)), lambda t: (piece7(t, 0), piece7(t, 1), attention_norm(t)),
                      piece8, piece9, lambda t: (piece10(t), residual(t, 0)), lambda t: (residual(t, 1), piece12(t)),
                      lambda t: None, lambda t: best_pair(t, 0), lambda t: (best_pair(t, 1), pick(t, 0, 4)),
                      lambda t: best_pair(t, 2),
                      lambda t: (best_pair(t, 3), pick(t, 4, 4), gates(t, 0, PH, vector_front), end_of_front()), lambda t: None]

            def publish(t):
                dve.wait_ge(vector_front, t + 1)
                dve.wait_ge(weights_ready, t * NG)
                v.tensor_copy(xb[:], xb_new[:])
                v.tensor_copy(gate[:], gate_new[:]).then_inc(inputs_ready, 1)
                dve.wait_ge(inputs_ready, t + 1)

            def experts(t, g):
                for j in range(G):
                    dve.wait_ge(u_landed[j], (t * NG + g + 1) * 16)
                    v.tensor_tensor_reduce(u_ring[:, j, :], u_ring[:, j, :], xb[:], 1.0, 0.0, ALU.mult, ALU.add,
                                                hid[:, g * G + j:g * G + j + 1]).then_inc(u_used, 1)
                dve.wait_ge(gelu, t * NG + g + 1)
                v.tensor_tensor(act_w[:, g * G:g * G + G], gel[:, g * G:g * G + G], gate[:, g * G:g * G + G], ALU.mult).then_inc(weights_ready, 1)

            def experts_out(t):
                dve.wait_ge(v_used, (t + 1) * SLOTS)
                for n in range(2):
                    v.tensor_copy(h2_sb[:, n * 512:n * 512 + 512], acc[:, n * 512:n * 512 + 512]).then_inc(h2_ready, 1)

            def tile(t):
                for g in range(NG):
                    experts(t - 1, g)
                    if g == 0:
                        experts_out(t - 2)
                    pieces[g](t)
                publish(t)

            for piece in pieces[:10]:
                piece(0)
            best_pair(0, 0)
            pick(0, 0, 2)
            gates(0, 0, 2, vector_step)
            dve.wait_ge(vector_step, steps(0))
            v.tensor_copy(xb[:], xb_new[:])
            v.tensor_copy(gate[:, 0:EARLY * G], gate_new[:, 0:EARLY * G]).then_inc(vector_step, 1)
            dve.wait_ge(vector_step, steps(0))
            best_pair(0, 1)
            pick(0, 2, 2)
            experts(0, 0)
            best_pair(0, 2)
            experts(0, 1)
            best_pair(0, 3)
            pick(0, 4, 4)
            gates(0, 2, PH, vector_front)
            assert counted[0] == V_STEPS + V_FIRST, counted
            counted[0] = 0
            dve.wait_ge(vector_front, 1)
            v.tensor_copy(gate[:, EARLY * G:SLOTS], gate_new[:, EARLY * G:SLOTS]).then_inc(inputs_ready, 1)
            dve.wait_ge(inputs_ready, 1)
            for i, group in enumerate(merged(pieces)):
                experts(0, FIRST + i)
                for piece in group:
                    piece(1)
            publish(1)
            with dve.Fori(2, NT) as t:
                tile(t)

            def normed_rows(k):
                dve.wait_ge(row_squares, 2 * NT + k + 1)
                mean_to_ms(c_rs, c_ss, D).then_inc(mean_square, 1)
                dve.wait_ge(root, 5 * NT + k + 1)
                v.reciprocal(c_rs, c_rs).then_inc(inverse_root, 1)
                dve.wait_ge(inverse_root, NT + k + 1)
                dve.wait_ge(n2_T, 2 * NT + 2 * k)
                v.scalar_tensor_tensor(c_n, ple_rows(k), c_rs, g_ple_b, ALU.mult, ALU.mult).then_inc(xb_ready, 1)

            def take_pT(k):
                dve.wait_ge(c_pT_turned, k + 1)
                v.tensor_copy(c_pT.rearrange("p c n -> p (c n)"), bank[2][:, 0:PLE]).then_inc(c_pT_ready, 1)

            def result(k):
                dve.wait_ge(rows_stored[k % 2], 8 * NT + (k // 2) * 16)
                dve.wait_ge(c_proj_mm, 2 * k + 2)
                dve.wait_ge(c_gate, 2 * k + 2)
                for n in range(2):
                    half = slice(n * 512, n * 512 + 512)
                    last = v.tensor_tensor(c_o[k % 2][:, half], c_e[:, half], bank[(5, 2)[n]][:, :], ALU.mult)
                last.then_inc(c_gated, 1)
                dve.wait_ge(c_gated, k + 1)
                v.tensor_tensor(c_o[k % 2], c_o[k % 2], ple_rows(k), ALU.add).then_inc(c_out_ready, 1)

            for g in range(NG):
                experts(NT - 1, g)
                k = (g - 1) // 2
                if g == 0:
                    experts_out(NT - 2)
                    dve.wait_ge(c_gain_loaded, 16)
                    normed_rows(0)
                elif g % 2:
                    if k:
                        result(k - 1)
                    take_pT(k)
                elif k + 1 < NT - 1:
                    normed_rows(k + 1)
            experts_out(NT - 1)
            normed_rows(NT - 1)
            result(NT - 1)


_INS = ["x", "p", "g_mix", "w_in", "gdn_conv_w", "gdn_a_log", "gdn_dt_bias", "gdn_norm_g", "swa_q_norm_g", "swa_k_norm_g",
        "swa_sinks", "rel_bias", "w_out", "g_ffn", "peer_w_query", "peer_sub_keys", "peer_u", "peer_v", "g_ple",
        "ple_w_gate", "ple_w_proj"]


def kernel(**inputs):
    import concourse.bacc as _bacc
    from concourse.bass_utils import run_bass_kernel_spmd as _run

    nc = _bacc.Bacc("TRN2", target_bir_lowering=False, num_devices=1)
    arrays, args = {}, []
    for name in _INS + ["consts"]:
        a = constants() if name == "consts" else np.ascontiguousarray(inputs[name])
        arrays[f"in_{name}_dram"] = a
        args.append(nc.dram_tensor(f"in_{name}_dram", a.shape, mybir.dt.from_np(a.dtype), kind="ExternalInput").ap())
    out = nc.dram_tensor("out_0_dram", (1, SEQ, D), F32, kind="ExternalOutput").ap()
    block_kernel(nc, *args, out)
    r = _run(nc, [arrays], core_ids=[0])
    return r.results[0]["out_0_dram"]
```
